# Optimizing a Trainium2 kernel written in Bass

```python
import jax
import jax.numpy as jnp
from jax import lax
import numpy as np

D_MODEL = 1024
BATCH = 1
SEQ = 1024
DEPTH = 2
DEC_BATCH = 8
DEC_SEQ = 1
PAST_LEN = 1024
PAGE_SIZE = 128

N_A_LAYERS = DEPTH // 2
N_B_LAYERS = DEPTH - N_A_LAYERS
D_RNN = D_MODEL
LRU_HEADS = 8
LRU_BLOCK = D_RNN // LRU_HEADS
LRU_CONV_W = 4
LRU_C = 8.0
N_HEADS = 16
HEAD_DIM = 64
N_KV_HEADS = 4
GROUP = N_HEADS // N_KV_HEADS
Q_WIDTH = N_HEADS * HEAD_DIM
L_CMP = 32
D_CMP = 16
CMP_HIDDEN = 128
L_SEL = 64
TOP_N = 8
WINDOW = 512
Q_BLOCK = 128
ROT_DIM = HEAD_DIM // 4
ROPE_THETA = 500000.0
N_KV_SLOTS = 4
D_FF = 3 * D_MODEL
FFN_CONV_W = 3
N_MOD = 6
EPS = 1e-6
NEG_INF = -1e30
FORCED_SCORE = 1e6

kernel_name = 'hawk_nsa_yoco_decode_step'

def rmsnorm(x, g):
    xf = x.astype(jnp.float32)
    y = xf * lax.rsqrt(jnp.mean(xf * xf, axis=-1, keepdims=True) + EPS)
    return (y * g.astype(jnp.float32)).astype(x.dtype)

def ada_mod(c, w, b, n):
    m = jax.nn.silu(c) @ w + b
    return m.reshape(c.shape[0], n, 1, D_MODEL)

def causal_dwconv(u, buf, w, b):
    t = u.shape[1]
    xp = jnp.concatenate([buf.astype(u.dtype), u], axis=1)
    out = b + sum(w[k] * xp[:, k:k + t] for k in range(w.shape[0]))
    return out, xp[:, t:]

def rope_partial(x, pos):
    half = ROT_DIM // 2
    inv = jnp.power(ROPE_THETA, -jnp.arange(half, dtype=jnp.float32) * (2.0 / ROT_DIM))
    ang = pos.astype(jnp.float32)[:, None] * inv[None, :]
    cos = jnp.cos(ang)[:, None, :].astype(x.dtype)
    sin = jnp.sin(ang)[:, None, :].astype(x.dtype)
    x1 = x[..., :half]
    x2 = x[..., half:ROT_DIM]
    return jnp.concatenate([x1 * cos - x2 * sin, x2 * cos + x1 * sin, x[..., ROT_DIM:]], axis=-1)

def masked_softmax(s, mask):
    s = jnp.where(mask, s, NEG_INF)
    p = jax.nn.softmax(s, axis=-1)
    return jnp.where(mask, p, 0.0)

def lru_combine(e1, e2):
    a1, b1 = e1
    a2, b2 = e2
    return a1 * a2, a2 * b1 + b2

def rglru_block(h, h0, conv_buf, w_in, b_in, w_conv, b_conv, w_gate, b_gate, lam, w_out):
    bsz, t, _ = h.shape
    proj = h @ w_in + b_in
    y_branch = jax.nn.gelu(proj[..., :D_RNN])
    u, new_buf = causal_dwconv(proj[..., D_RNN:], conv_buf, w_conv, b_conv)
    ub = u.reshape(bsz, t, LRU_HEADS, LRU_BLOCK)
    gates = jnp.einsum('bthi,ghij->gbthj', ub, w_gate).reshape(2, bsz, t, D_RNN) + b_gate[:, None, None, :]
    r = jax.nn.sigmoid(gates[0].astype(jnp.float32))
    i = jax.nn.sigmoid(gates[1].astype(jnp.float32))
    log_a = -LRU_C * r * jax.nn.softplus(-lam.astype(jnp.float32))
    a = jnp.exp(log_a)
    bx = jnp.sqrt(-jnp.expm1(2.0 * log_a)) * (i * u.astype(jnp.float32))
    bx = bx.at[:, 0].add(a[:, 0] * h0.astype(jnp.float32))
    _, hs = lax.associative_scan(lru_combine, (a, bx), axis=1)
    out = (hs.astype(h.dtype) * y_branch) @ w_out
    return out, hs[:, -1].astype(h.dtype), new_buf

def conv_ffn(h, buf, w_in, w_conv, b_conv, w_out):
    z, new_buf = causal_dwconv(h @ w_in, buf, w_conv, b_conv)
    return (jax.nn.gelu(z[..., :D_FF]) * z[..., D_FF:]) @ w_out, new_buf

def shared_kv(x, c, pos, g_kv, w_mod_kv, b_mod_kv, w_kv):
    bsz, t, _ = x.shape
    m = ada_mod(c, w_mod_kv, b_mod_kv, 2)
    h = rmsnorm(x, g_kv) * (1.0 + m[:, 1]) + m[:, 0]
    kv = (h @ w_kv).reshape(bsz, t, 6, N_KV_HEADS, HEAD_DIM)
    rows = jnp.stack([kv[:, :, 0], kv[:, :, 1], rope_partial(kv[:, :, 2], pos), kv[:, :, 3]], axis=2)
    win = jnp.stack([rope_partial(kv[:, :, 4], pos), kv[:, :, 5]], axis=2)
    return rows, win

def compress(seq_rows, pe, w1, b1, w2):
    bsz, t = seq_rows.shape[:2]
    nc = (t - L_CMP) // D_CMP + 1
    idx = np.arange(nc)[:, None] * D_CMP + np.arange(L_CMP)[None, :]
    blk = seq_rows[:, idx] + pe[None, None, :, None, :]
    blk = blk.transpose(0, 1, 3, 2, 4).reshape(bsz, nc, N_KV_HEADS, L_CMP * HEAD_DIM)
    return jax.nn.gelu(blk @ w1 + b1) @ w2

def sel_blocks(seq_rows, ns):
    bsz, t = seq_rows.shape[:2]
    xp = jnp.pad(seq_rows, ((0, 0), (0, ns * L_SEL - t), (0, 0), (0, 0)))
    return xp.reshape(bsz, ns, L_SEL, N_KV_HEADS, HEAD_DIM).transpose(0, 3, 1, 2, 4)

def nsa_context(rows, pe_cmp, w_cmp1, b_cmp1, w_cmp2):
    t = rows.shape[1]
    nc = (t - L_CMP) // D_CMP + 1
    ns = -(-t // L_SEL)
    c_start = np.arange(nc) * D_CMP
    s_start = np.arange(ns) * L_SEL
    cmp_to_sel = ((c_start[:, None] < s_start[None, :] + L_SEL)
                  & (c_start[:, None] + L_CMP > s_start[None, :])).astype(np.float32)
    return {
        'kc': compress(rows[:, :, 0], pe_cmp[0], w_cmp1[0], b_cmp1[0], w_cmp2[0]),
        'vc': compress(rows[:, :, 1], pe_cmp[1], w_cmp1[1], b_cmp1[1], w_cmp2[1]),
        'cend': jnp.asarray(c_start + L_CMP - 1, dtype=jnp.int32),
        'ks': sel_blocks(rows[:, :, 2], ns),
        'vs': sel_blocks(rows[:, :, 3], ns),
        'cmp_to_sel': jnp.asarray(cmp_to_sel),
    }

def nsa_attend(q_rot, q_raw, gates, q_pos, ctx, kw, vw, kw_pos):
    bsz, nq = q_rot.shape[:2]
    scale = HEAD_DIM ** -0.5
    qr = q_raw.reshape(bsz, nq, N_KV_HEADS, GROUP, HEAD_DIM)
    qs = q_rot.reshape(bsz, nq, N_KV_HEADS, GROUP, HEAD_DIM)
    s_c = jnp.einsum('bcgrd,bngd->bcgrn', qr, ctx['kc']).astype(jnp.float32) * scale
    m_c = (ctx['cend'][None, :] <= q_pos[:, None])[None, :, None, None, :]
    p_c = masked_softmax(s_c, m_c)
    o_c = jnp.einsum('bcgrn,bngd->bcgrd', p_c, ctx['vc'].astype(jnp.float32))
    ns = ctx['ks'].shape[2]
    imp = jnp.einsum('bcgrn,nj->bcgj', p_c, ctx['cmp_to_sel'])
    blk = jnp.arange(ns)[None, :]
    cur = (q_pos // L_SEL)[:, None]
    forced = (blk == 0) | (blk == cur) | (blk == cur - 1)
    imp = jnp.where(forced[None, :, None, :], FORCED_SCORE, imp)
    imp = jnp.where((blk <= cur)[None, :, None, :], imp, NEG_INF)
    n_top = min(TOP_N, ns)
    top_val, top_idx = lax.top_k(imp, n_top)
    b_ix = jnp.arange(bsz)[:, None, None, None]
    g_ix = jnp.arange(N_KV_HEADS)[None, None, :, None]
    n_sel = n_top * L_SEL
    k_g = ctx['ks'][b_ix, g_ix, top_idx].reshape(bsz, nq, N_KV_HEADS, n_sel, HEAD_DIM)
    v_g = ctx['vs'][b_ix, g_ix, top_idx].reshape(bsz, nq, N_KV_HEADS, n_sel, HEAD_DIM)
    k_pos = top_idx[..., None] * L_SEL + jnp.arange(L_SEL)
    m_s = ((top_val > 0.5 * NEG_INF)[..., None]
           & (k_pos <= q_pos[None, :, None, None, None])).reshape(bsz, nq, N_KV_HEADS, 1, n_sel)
    s_s = jnp.einsum('bcgrd,bcgkd->bcgrk', qs, k_g).astype(jnp.float32) * scale
    p_s = masked_softmax(s_s, m_s)
    o_s = jnp.einsum('bcgrk,bcgkd->bcgrd', p_s, v_g.astype(jnp.float32))
    dpos = q_pos[:, None] - kw_pos[None, :]
    m_w = ((kw_pos[None, :] >= 0) & (dpos >= 0) & (dpos < WINDOW))[None, :, None, None, :]
    s_w = jnp.einsum('bcgrd,bkgd->bcgrk', qs, kw).astype(jnp.float32) * scale
    p_w = masked_softmax(s_w, m_w)
    o_w = jnp.einsum('bcgrk,bkgd->bcgrd', p_w, vw.astype(jnp.float32))
    g = gates.reshape(bsz, nq, N_KV_HEADS, GROUP, 3)
    o = g[..., 0:1] * o_c + g[..., 1:2] * o_s + g[..., 2:3] * o_w
    return o.reshape(bsz, nq, Q_WIDTH)

def nsa_mix(h, q_pos, ctx, w_qg, w_o, banded):
    bsz, t, _ = h.shape
    proj = h @ w_qg
    q = proj[..., :Q_WIDTH].reshape(bsz, t, N_HEADS, HEAD_DIM)
    gates = jax.nn.sigmoid(proj[..., Q_WIDTH:].astype(jnp.float32)).reshape(bsz, t, N_HEADS, 3)
    q_rot = rope_partial(q, q_pos)
    if banded:
        nblk = t // Q_BLOCK
        kw_pad = jnp.pad(ctx['kw'], ((0, 0), (WINDOW, 0), (0, 0), (0, 0)))
        vw_pad = jnp.pad(ctx['vw'], ((0, 0), (WINDOW, 0), (0, 0), (0, 0)))

        def to_blocks(a):
            return a.reshape((bsz, nblk, Q_BLOCK) + a.shape[2:]).swapaxes(0, 1)

        def one_block(args):
            i, qr_b, qx_b, g_b, p_b = args
            start = i * Q_BLOCK
            kw = lax.dynamic_slice_in_dim(kw_pad, start, WINDOW + Q_BLOCK, axis=1)
            vw = lax.dynamic_slice_in_dim(vw_pad, start, WINDOW + Q_BLOCK, axis=1)
            kw_pos = start - WINDOW + jnp.arange(WINDOW + Q_BLOCK)
            return nsa_attend(qr_b, qx_b, g_b, p_b, ctx, kw, vw, kw_pos)

        o = lax.map(one_block, (jnp.arange(nblk), to_blocks(q_rot), to_blocks(q), to_blocks(gates),
                                q_pos.reshape(nblk, Q_BLOCK)))
        o = o.swapaxes(0, 1).reshape(bsz, t, Q_WIDTH)
    else:
        o = nsa_attend(q_rot, q, gates, q_pos, ctx, ctx['kw'], ctx['vw'], ctx['kw_pos'])
    return o.astype(h.dtype) @ w_o

def trunk(x, c, pos, lru_h0, lru_conv0, ffn_conv0, build_ctx, banded, lw):
    lru_h, lru_conv, ffn_conv = [], [], []
    ctx, kv_state = None, None
    for l in range(DEPTH):
        m = ada_mod(c, lw['w_mod'][l], lw['b_mod'][l], N_MOD)
        g = lw['g_norm'][l]
        h = rmsnorm(x, g[0]) * (1.0 + m[:, 1]) + m[:, 0]
        if l < N_A_LAYERS:
            o, h_last, cbuf = rglru_block(h, lru_h0[l], lru_conv0[l], lw['w_lru_in'][l], lw['b_lru_in'][l],
                                          lw['w_lru_conv'][l], lw['b_lru_conv'][l], lw['w_lru_gate'][l],
                                          lw['b_lru_gate'][l], lw['lru_lambda'][l], lw['w_lru_out'][l])
            lru_h.append(h_last)
            lru_conv.append(cbuf)
        else:
            j = l - N_A_LAYERS
            o = nsa_mix(h, pos, ctx, lw['w_nsa_qg'][j], lw['w_nsa_out'][j], banded)
        x = x + m[:, 2] * rmsnorm(o, g[1])
        h = rmsnorm(x, g[2]) * (1.0 + m[:, 4]) + m[:, 3]
        o, fbuf = conv_ffn(h, ffn_conv0[l], lw['w_ffn_in'][l], lw['w_ffn_conv'][l], lw['b_ffn_conv'][l],
                           lw['w_ffn_out'][l])
        ffn_conv.append(fbuf)
        x = x + m[:, 5] * rmsnorm(o, g[3])
        if l == N_A_LAYERS - 1:
            ctx, kv_state = build_ctx(x, c)
    return x, kv_state, jnp.stack(lru_h), jnp.stack(lru_conv), jnp.stack(ffn_conv)

def setup_inputs(seed: int = 0) -> dict:
    key = jax.random.key(seed)
    ks = iter(jax.random.split(key, 48))

    def nrm(shape, s):
        return jax.random.normal(next(ks), shape, jnp.float32) * s

    n_pages = PAST_LEN // PAGE_SIZE
    n_phys = (DEC_BATCH * n_pages * 5) // 4
    perm = jax.random.permutation(next(ks), n_phys)
    page_table = perm[:DEC_BATCH * n_pages].reshape(DEC_BATCH, n_pages).astype(jnp.int32)
    win_buf = min(WINDOW, PAST_LEN)
    a0 = jax.random.uniform(next(ks), (N_A_LAYERS, D_RNN), jnp.float32, 0.9, 0.999)
    lru_lambda = jnp.log(a0) - jnp.log1p(-a0)
    d_inv = D_MODEL ** -0.5
    return {
        'x_prompt': nrm((BATCH, SEQ, D_MODEL), 1.0),
        'x_sample': nrm((DEC_BATCH, DEC_SEQ, D_MODEL), 1.0),
        'c_prompt': nrm((BATCH, D_MODEL), 1.0),
        'c_sample': nrm((DEC_BATCH, D_MODEL), 1.0),
        'cache_nsa_kv': nrm((n_phys, PAGE_SIZE, N_KV_SLOTS, N_KV_HEADS, HEAD_DIM), 1.0),
        'page_table': page_table,
        'state_nsa_win': nrm((DEC_BATCH, win_buf, 2, N_KV_HEADS, HEAD_DIM), 1.0),
        'state_lru_h': nrm((N_A_LAYERS, DEC_BATCH, D_RNN), 0.5),
        'state_lru_conv': nrm((N_A_LAYERS, DEC_BATCH, LRU_CONV_W - 1, D_RNN), 1.0),
        'state_ffn_conv': nrm((DEPTH, DEC_BATCH, FFN_CONV_W - 1, 2 * D_FF), 1.0),
        'w_mod': nrm((DEPTH, D_MODEL, N_MOD * D_MODEL), 0.5 * d_inv),
        'b_mod': nrm((DEPTH, N_MOD * D_MODEL), 0.01),
        'g_norm': 1.0 + nrm((DEPTH, 4, D_MODEL), 0.02),
        'w_lru_in': nrm((N_A_LAYERS, D_MODEL, 2 * D_RNN), d_inv),
        'b_lru_in': nrm((N_A_LAYERS, 2 * D_RNN), 0.01),
        'w_lru_conv': nrm((N_A_LAYERS, LRU_CONV_W, D_RNN), LRU_CONV_W ** -0.5),
        'b_lru_conv': nrm((N_A_LAYERS, D_RNN), 0.01),
        'w_lru_gate': nrm((N_A_LAYERS, 2, LRU_HEADS, LRU_BLOCK, LRU_BLOCK), LRU_BLOCK ** -0.5),
        'b_lru_gate': nrm((N_A_LAYERS, 2, D_RNN), 0.01),
        'lru_lambda': lru_lambda,
        'w_lru_out': nrm((N_A_LAYERS, D_RNN, D_MODEL), D_RNN ** -0.5),
        'g_kv': 1.0 + nrm((D_MODEL,), 0.02),
        'w_mod_kv': nrm((D_MODEL, 2 * D_MODEL), 0.5 * d_inv),
        'b_mod_kv': nrm((2 * D_MODEL,), 0.01),
        'w_kv': nrm((D_MODEL, 6 * N_KV_HEADS * HEAD_DIM), d_inv),
        'pe_cmp': nrm((2, L_CMP, HEAD_DIM), 0.1),
        'w_cmp1': nrm((2, L_CMP * HEAD_DIM, CMP_HIDDEN), (L_CMP * HEAD_DIM) ** -0.5),
        'b_cmp1': nrm((2, CMP_HIDDEN), 0.01),
        'w_cmp2': nrm((2, CMP_HIDDEN, HEAD_DIM), CMP_HIDDEN ** -0.5),
        'w_nsa_qg': nrm((N_B_LAYERS, D_MODEL, Q_WIDTH + 3 * N_HEADS), d_inv),
        'w_nsa_out': nrm((N_B_LAYERS, Q_WIDTH, D_MODEL), Q_WIDTH ** -0.5),
        'w_ffn_in': nrm((DEPTH, D_MODEL, 2 * D_FF), d_inv),
        'w_ffn_conv': nrm((DEPTH, FFN_CONV_W, 2 * D_FF), FFN_CONV_W ** -0.5),
        'b_ffn_conv': nrm((DEPTH, 2 * D_FF), 0.01),
        'w_ffn_out': nrm((DEPTH, D_FF, D_MODEL), D_FF ** -0.5),
    }

def reference(x_prompt, x_sample, c_prompt, c_sample, cache_nsa_kv, page_table, state_nsa_win,
              state_lru_h, state_lru_conv, state_ffn_conv, w_mod, b_mod, g_norm,
              w_lru_in, b_lru_in, w_lru_conv, b_lru_conv, w_lru_gate, b_lru_gate, lru_lambda, w_lru_out,
              g_kv, w_mod_kv, b_mod_kv, w_kv, pe_cmp, w_cmp1, b_cmp1, w_cmp2,
              w_nsa_qg, w_nsa_out, w_ffn_in, w_ffn_conv, b_ffn_conv, w_ffn_out):
    lw = {'w_mod': w_mod, 'b_mod': b_mod, 'g_norm': g_norm, 'w_lru_in': w_lru_in, 'b_lru_in': b_lru_in,
          'w_lru_conv': w_lru_conv, 'b_lru_conv': b_lru_conv, 'w_lru_gate': w_lru_gate,
          'b_lru_gate': b_lru_gate, 'lru_lambda': lru_lambda, 'w_lru_out': w_lru_out,
          'w_nsa_qg': w_nsa_qg, 'w_nsa_out': w_nsa_out, 'w_ffn_in': w_ffn_in,
          'w_ffn_conv': w_ffn_conv, 'b_ffn_conv': b_ffn_conv, 'w_ffn_out': w_ffn_out}

    bsz_p, t_p, _ = x_prompt.shape
    pos_p = jnp.arange(t_p, dtype=jnp.int32)

    def prompt_ctx(x, c):
        rows, win = shared_kv(x, c, pos_p, g_kv, w_mod_kv, b_mod_kv, w_kv)
        ctx = nsa_context(rows, pe_cmp, w_cmp1, b_cmp1, w_cmp2)
        ctx.update(kw=win[:, :, 0], vw=win[:, :, 1], kw_pos=pos_p)
        return ctx, (rows, win[:, t_p - min(WINDOW, t_p):])

    dt = x_prompt.dtype
    y_prompt, (rows_p, win_p), lh_p, lc_p, fc_p = trunk(
        x_prompt, c_prompt, pos_p,
        jnp.zeros((N_A_LAYERS, bsz_p, D_RNN), dt),
        jnp.zeros((N_A_LAYERS, bsz_p, LRU_CONV_W - 1, D_RNN), dt),
        jnp.zeros((DEPTH, bsz_p, FFN_CONV_W - 1, 2 * D_FF), dt),
        prompt_ctx, True, lw)

    bsz_s, t_s, _ = x_sample.shape
    pos_s = PAST_LEN + jnp.arange(t_s, dtype=jnp.int32)

    def sample_ctx(x, c):
        rows, win = shared_kv(x, c, pos_s, g_kv, w_mod_kv, b_mod_kv, w_kv)
        n_pages = page_table.shape[1]
        past = cache_nsa_kv[page_table].reshape((bsz_s, n_pages * PAGE_SIZE) + cache_nsa_kv.shape[2:])
        full = jnp.concatenate([past.astype(rows.dtype), rows], axis=1)
        ctx = nsa_context(full, pe_cmp, w_cmp1, b_cmp1, w_cmp2)
        win_buf = state_nsa_win.shape[1]
        win_all = jnp.concatenate([state_nsa_win.astype(win.dtype), win], axis=1)
        kw_pos = PAST_LEN - win_buf + jnp.arange(win_buf + t_s, dtype=jnp.int32)
        ctx.update(kw=win_all[:, :, 0], vw=win_all[:, :, 1], kw_pos=kw_pos)
        keep = min(WINDOW, PAST_LEN + t_s)
        return ctx, (rows, win_all[:, win_buf + t_s - keep:])

    y_sample, (rows_s, win_s), lh_s, lc_s, fc_s = trunk(
        x_sample, c_sample, pos_s, state_lru_h, state_lru_conv, state_ffn_conv,
        sample_ctx, False, lw)

    return (y_prompt, y_sample, rows_p, rows_s, win_p, win_s, lh_p, lh_s, lc_p, lc_s, fc_p, fc_s)


_drawn_inputs = setup_inputs


def setup_inputs(seed=0):
    import zlib

    import numpy as np

    out = dict(_drawn_inputs(seed))
    spreads = {}
    factors = {'b_lru_gate': 8.0, 'g_kv': 2.786, 'b_mod_kv': 4.431, 'b_cmp1': 8.0, 'b_ffn_conv': 6.593}
    for name, (base, spread) in spreads.items():
        noise = np.random.default_rng([zlib.crc32(name.encode()), seed]).standard_normal(out[name].shape)
        drawn = base * np.exp(spread * noise) if base else spread * noise
        out[name] = jnp.asarray(drawn.astype(out[name].dtype))
    for name, factor in factors.items():
        out[name] = (out[name] * factor).astype(out[name].dtype)
    return out
```

```python
import numpy as np
import concourse.bass as bass
from concourse import mybir

F32 = mybir.dt.float32
F32R = mybir.dt.float32r
I32 = mybir.dt.int32
ALU = mybir.AluOpType
ACT = mybir.ActivationFunctionType
AXX = mybir.AxisListType.X
ds = bass.ds

P = 128
D = 1024
KT = D // P
NPR = 1024
NS = 8
TOK = NPR + NS
NCH = 3
CH = TOK // NCH
NC = 1 + NS
DFF = 3 * D
FT = DFF // P
PAIRS = 4
CHUNKS = FT // PAIRS
LRU_W = 4
EPS = 1e-6
QT = NPR // P
NEG = -1e30
FORCED = 1e6
TAKEN = -3e38
PAST = 1024
PAGES = 8
NPHYS = 80
NCMP = 63
SCALE = 0.125

_names = [("b_mod", 112), ("g_norm", 72), ("b_lru_in", 16), ("w_lru_conv", 32), ("b_lru_conv", 8),
          ("b_lru_gate", 16), ("lam", 8), ("w_ffn_conv", 288), ("b_ffn_conv", 96), ("b_cmp1", 2)]
VC, _at = {}, 0
for _n, _w in _names:
    VC[_n] = _at
    _at += _w
NV = _at

T_LRU, T_LRUO, T_FFN0 = 0, 16, 24
T_KV = T_FFN0 + 72
T_Q = T_KV + 12
T_O = T_Q + 9
T_FFN1 = T_O + 8
NW = T_FFN1 + 72


def c3(ap):
    return ap.rearrange("p (c n) -> p c n", c=NCH)


def after(eng, sem, count):
    if not (isinstance(count, int) and count <= 0):
        eng.wait_ge(sem, count)


def rolled(eng, first, last, body):
    body(first)
    if last - first == 2:
        body(first + 1)
    elif last - first > 2:
        with eng.Fori(first + 1, last) as i:
            body(i)


def build(nc, a, o):
    base = 16512
    at = [base]

    def sb(name, shape, dt=F32, offset=None):
        size = 4 * int(np.prod(shape[1:]))
        if offset is None:
            offset = at[0]
            at[0] += (size + 31) // 32 * 32
        return nc.alloc_sbuf_tensor_at(name, shape, dt, offset=offset).ap()

    REG = 4 * KT * TOK
    reg = [base + i * REG for i in range(5)]
    at[0] = base + 5 * REG
    w_raw = [sb(f"w_raw{i}", [P, 1024]) for i in range(2)]
    w_hi = [sb(f"w_hi{i}", [P, 1024], F32R) for i in range(2)]
    w_lo = [sb(f"w_lo{i}", [P, 1024], F32R) for i in range(2)]
    modT = sb("modT", [P, 112, NC])
    vec = sb("vec", [P, NV])
    ident = sb("ident", [P, P])
    ones = sb("ones", [P, P])
    perm = sb("perm", [P, P])
    spots = {"rms": at[0]}
    rms = sb("rms", [P, TOK])
    cosT = sb("cosT", [P, TOK])
    sinT = sb("sinT", [P, TOK])
    ts = sb("ts", [P, KT, NS])
    sp2 = sb("sp2", [P, KT])
    misc = sb("misc", [P, 8])
    deps, zero, nm0 = misc[:, 0:1], misc[:, 1:2], misc[:, 2:3]
    mark, dmark, pmark = misc[0:1, 3:4], misc[0:1, 4:5], misc[0:1, 5:6]
    k_new = sb("k_new", [P, 2, 2, NS])
    v_new = sb("v_new", [NS, 2, 256])
    assert at[0] <= 229368, at[0]

    def view(name, region, shape, dt=F32, at_byte=0):
        assert at_byte + 4 * int(np.prod(shape[1:])) <= REG * 5
        return sb(name, shape, dt, offset=reg[region] + at_byte)

    def pack(names, region):
        out, off = {}, 0
        for n, shape, dt in names:
            out[n] = view(n, region, shape, dt, off)
            off += (4 * int(np.prod(shape[1:])) + 31) // 32 * 32
        assert off <= REG, off
        return out

    X = view("X", 4, [P, KT, TOK])
    HA = [view("hA_hi", 1, [P, KT, TOK], F32R), view("hA_lo", 2, [P, KT, TOK], F32R)]
    SS = [view("s_hi", 0, [P, KT, TOK], F32R), view("s_lo", 3, [P, KT, TOK], F32R)]
    HB = [view("hB_hi", 2, [P, KT, TOK], F32R), view("hB_lo", 3, [P, KT, TOK], F32R)]
    Y = view("gelu_y", 3, [P, KT, TOK])
    O1 = view("O1", 1, [P, KT, TOK])
    O0 = view("O0", 0, [P, KT, TOK])
    G = [view("g_hi", 1, [P, PAIRS, TOK], F32R), view("g_lo", 1, [P, PAIRS, TOK], F32R, REG // 2)]
    mw = [view("mw0", 0, [P, 4096]), view("mw1", 0, [P, 4096], F32, 16384), view("mw2", 1, [P, 4096]),
          view("mw3", 4, [P, 4096], F32, REG // 2)]
    mw_hi = view("mw_hi", 2, [P, 2, 4096], F32R)
    mw_lo = view("mw_lo", 3, [P, 2, 4096], F32R)
    mrow = view("mrow", 1, [2 * NC, 2, 512], F32, 16384)
    csplit = view("csplit", 1, [P, KT, 2 * NC], F32R, 24576)
    fold = view("fold", 1, [2 * NC, NC], F32, 28672)
    cT = view("cT", 1, [P, KT * NC], F32, 20480)
    csil = view("csil", 1, [P, KT, NC], F32, 22528)

    def norm_bufs(region):
        return pack([(f"{n}_{region}", [P, TOK], F32) for n in ("sq0", "sq1", "t0", "t1", "h0", "h1")], region)

    NB = {r: norm_bufs(r) for r in (0, 1, 2)}
    F = pack([("ua", [P, TOK + 2], F32), ("ub", [P, TOK + 2], F32), ("za", [P, TOK], F32), ("zb", [P, TOK], F32),
              ("gel", [P, TOK], F32), ("g32", [P, TOK], F32), ("fst", [P, 48, 2, NS], F32),
              ("fsc", [P, 48, NS], F32), ("utail", [P, 48, 10], F32)], 4)
    L = pack([("lu", [P, TOK + 3], F32), ("uc", [P, TOK], F32), ("hs", [P, TOK], F32), ("tr", [P, TOK], F32),
              ("ti", [P, TOK], F32), ("lq", [P, TOK], F32), ("am", [P, TOK], F32), ("gw", [P, 256], F32),
              ("lst", [P, KT, 3, NS], F32), ("lh0", [P, KT, NS], F32), ("lsc", [P, KT, NS], F32),
              ("ltail", [P, KT, 11], F32), ("hlast", [P, KT, NC], F32)], 4)

    def kvbuf(name, shape, dt, off):
        return view(name, 0, shape, dt, off)

    K2 = [kvbuf("k2_k", [P, 8, 4, 64], F32, 0), kvbuf("k2_v", [P, 8, 4, 64], F32, 8192)]
    KBD = [kvbuf("kbd_sel", [P, 2, 2, NPR], F32, 16384), kvbuf("kbd_win", [P, 2, 2, NPR], F32, 32768)]
    VT = [kvbuf("v_sel", [P, QT, 256], F32, 49152), kvbuf("v_win", [P, QT, 256], F32, 57344)]
    kb = [view(f"kb{i}", 4, [P, TOK], F32, i * 4 * TOK) for i in range(2)]
    kr = view("kr", 4, [P, TOK], F32, 8 * TOK)
    kx = view("kx", 4, [P, TOK], F32, 12 * TOK)
    aw = [base + 5 * REG]

    def awbuf(name, shape, dt=F32):
        ap = sb(name, shape, dt, offset=aw[0])
        aw[0] += (4 * int(np.prod(shape[1:])) + 31) // 32 * 32
        assert aw[0] <= base + 5 * REG + 24576
        return ap

    selm = awbuf("selm", [P, 4, QT, 16])
    gtok = awbuf("gtok", [P, QT, 48])
    gsmp = awbuf("gsmp", [NS, 48])
    wmask = awbuf("wmask", [P, 640])
    qc = [awbuf(f"qc{i}", [P, NPR]) for i in range(2)]
    pt = [awbuf(f"pt{i}", [P, 512]) for i in range(3)]
    gcur = awbuf("gcur", [P, QT, 2, 2, 2])
    nmx = [awbuf(f"nmx{i}", [P, 1]) for i in range(5)]
    psm = [awbuf(f"psm{i}", [P, 1]) for i in range(5)]
    pbuf = [kvbuf(f"pbuf{i}", [P, NPR], F32, 4096 * i) for i in range(4)] + [view("pbuf4", 3, [P, NPR], F32, 28672)]
    C = pack([("w1k", [P, 16, P], F32), ("w1v", [P, 16, P], F32), ("w2", [P, 2, 64], F32), ("pe", [P, 2, 16], F32),
              ("hid", [P, 2, 4, 64], F32), ("kc", [P, 2, 2, 64], F32), ("vc", [P, 2, P], F32),
              ("cadd", [P, QT, 64], F32), ("cmul", [P, QT, 64], F32), ("m1", [P, QT, 16], F32), ("m2", [P, QT, 16], F32),
              ("im0", [P, 2, 64], F32), ("im", [P, 2, 16], F32), ("top", [P, 2, 8], F32), ("im2", [P, 2, 16], F32),
              ("cm", [P, 8], F32), ("cs", [P, 8], F32), ("ct", [P, 4, P], F32)], 3)
    C["b1c"] = misc[:, 6:8]
    rx = view("rx", 3, [P, TOK])
    OC = view("oc", 2, [P, KT, TOK])

    vall = view("vall", 0, [P, NS, PAGES, 256])
    sbuf_s = [view(f"pages{i}", 3 + i, [P, PAGES, 768]) for i in range(2)]
    skw = [view(f"kwin{i}", 3 + i, [P, 2, 512], F32, 24576) for i in range(2)]
    vwin = view("vwin", 3, [P, NS, 4, 256])
    pT = view("pT", 4, [P, 13, P])
    pnT = view("pnT", 4, [NS, 2, P], F32, 13 * 512)
    s_s = view("s_s", 4, [P, 1025], F32, 28672)
    spot = [at[0]]
    at[0] = base + 5 * REG + 24576

    def run_of(start, limit, items):
        off = start
        out = []
        for n, shape, dt in items:
            out.append(sb(n, shape, dt, offset=off))
            off += (4 * int(np.prod(shape[1:])) + 31) // 32 * 32
        assert off <= limit, (off, limit)
        return out

    (sw1k, sw2, sE, kcs, s_c, s_hm, s_smp, sg48, sgate, snm, ssum, sim_, stop_, sim2, ssel, pnew, ptab) = run_of(
        spots["rms"], spots["rms"] + 3 * 4128,
        [("sw1k", [P, 16, P], F32), ("sw2", [P, 2, 64], F32), ("sE", [NS, P], F32), ("kcs", [P, 2, 63], F32), ("s_c", [P, 64], F32),
         ("s_hm", [P, 16], F32), ("s_smp", [P, NS], F32), ("sg48", [P, 3, 16], F32), ("sgate", [P, 3], F32), ("snm", [P, 3], F32),
         ("ssum", [P, 3], F32), ("sim_", [P, 17], F32), ("stop_", [P, 8], F32), ("sim2", [P, 17], F32), ("ssel", [P, 17], F32),
         ("pnew", [P, 2, NS], F32), ("ptab", [1, NS * PAGES], I32)])
    aw0 = base + 5 * REG
    sw1v, vcs, qp0, qp1 = run_of(aw0 + 3776, aw0 + 24576, [("sw1v", [P, 16, P], F32), ("vcs", [P, NS, 256], F32),
                                                           ("qpad0", [P, NS, 2, 32], F32), ("qpad1", [P, NS, 2, 32], F32)])
    qpad = [qp0, qp1]
    shid = sb("shid", [P, 2, 4, 64], offset=aw0)
    s_w = sb("s_w", [P, 513], offset=aw0 + 3776 + 2 * 8192)

    PA = nc.alloc_psum_tensor("PA", [P, NCH, 512], F32).ap()
    PB = nc.alloc_psum_tensor("PB", [P, NCH, 512], F32).ap()
    PC = nc.alloc_psum_tensor("PC", [P, 512], F32).ap()
    PD = nc.alloc_psum_tensor("PD", [P, 512], F32).ap()
    PS = [PA, PB]


    S = {}

    def sem(n):
        if n not in S:
            S[n] = nc.alloc_semaphore(n)
        return S[n]


    x_dram = nc.dram_tensor("x_dram", [P, KT * TOK], F32, kind="Internal").ap()
    block = nc.Block()
    block.__enter__()

    def mcol(slot, c):
        return modT[:, slot * KT + c, 0:1]

    def msamp(slot):
        return modT[:, slot * KT:(slot + 1) * KT, 1:NC]

    def v(name, c):
        if isinstance(c, int):
            return vec[:, VC[name] + c:VC[name] + c + 1]
        return vec[:, ds(c + VC[name], 1)]

    def vb(name, c, n, inner):
        return vec[:, VC[name] + c:VC[name] + c + n].unsqueeze(2).broadcast_to([P, n, inner])

    def flat(ap):
        return ap if ap.ndim == 2 else ap.rearrange({3: "p a b -> p (a b)", 4: "p a b c -> p (a b c)"}[ap.ndim])

    def kslice(ap, k):
        return ap[:, k, :] if isinstance(k, int) else ap[:, ds(k, 1), :].rearrange("p o n -> p (o n)")


    NREG = {0: 0, 1: 0, 2: 0, 3: 2, 4: 1, 5: 0, 6: 0, 7: 2}
    FFN_EV = {0: 24, 1: 72 + 12 + 9 + 8}
    FFN_DONE = {0: 24, 1: 149}

    def ffn_vec(l, name, k, f):
        return v(name, f + (l * 144 + k * 48 if name == "w_ffn_conv" else l * 48))

    def ffn_act(act, l):
        E0, D0, t0 = FFN_EV[l], FFN_DONE[l], (T_FFN0, T_FFN1)[l]
        act.wait_ge(sem("ffn_prep"), l + 1)

        def pair(c, p):
            n = c * PAIRS + (p + FT * l)
            f = c * PAIRS + p
            d = c * 16 + (D0 + 2 * p) if p == 0 else c * 16 + (D0 + 2 * p)
            for b, (u, z) in enumerate((("ua", "za"), ("ub", "zb"))):
                if p == 0:
                    act.wait_ge(sem("tile_done"), c * 16 + (D0 + b + 1) - 8 * (0 if isinstance(c, int) and c == 0 else 1))
                else:
                    act.wait_ge(sem("tile_done"), c * 16 + (D0 + 2 * p + b + 1))
                after(act, sem("conv_done"), n * 2 - (1 - b))
                if b == 0:
                    after(act, sem("g_ready"), n)
                act.activation(c3(F[u][:, 2:2 + TOK]), PS[(D0 + b) % 2][:, :, 0:CH], ACT.Copy)
                act.activation(c3(F[z]), PS[(D0 + b) % 2][:, :, 0:CH], ACT.Identity, bias=ffn_vec(l, "b_ffn_conv", 0, f + b * FT),
                               scale=ffn_vec(l, "w_ffn_conv", 2, f + b * FT)).then_inc(sem("ev_act"), 1)
            act.wait_ge(sem("conv_done"), n * 2 + 1)
            act.activation(F["gel"], F["za"], ACT.Gelu_apprx_tanh).then_inc(sem("gelu_ready"), 1)

        rolled(act, 0, CHUNKS, lambda c: [pair(c, p) for p in range(PAIRS)])

    def ffn_dve(dve, l):
        t0 = (T_FFN0, T_FFN1)[l]
        D0 = FFN_DONE[l]
        dve.wait_ge(sem("x_spill"), (16, 48)[l])
        dve.memset(F["ua"][:, 0:2], 0.0)
        dve.memset(F["ub"][:, 0:2], 0.0)
        dve.wait_ge(sem("st_in"), 32 + 16 * (l + 1))
        fst, fsc = F["fst"], F["fsc"]
        tmp = F["g32"][:, 0:48 * NS].rearrange("p (a b) -> p a b", b=NS)
        dve.tensor_tensor(fsc, fst[:, :, 0, :], vb("w_ffn_conv", l * 144, 48, NS), ALU.mult)
        dve.tensor_tensor(tmp, fst[:, :, 1, :], vb("w_ffn_conv", l * 144 + 48, 48, NS), ALU.mult)
        dve.drain()
        dve.tensor_tensor(fsc, fsc, tmp, ALU.add)
        dve.drain()
        dve.tensor_tensor(fsc, fsc, vb("b_ffn_conv", l * 48, 48, NS), ALU.add).then_inc(sem("ffn_prep"), 1)
        dve.drain()

        def conv(c, p, n, f):
            for b, (u, z) in enumerate(((F["ua"], F["za"]), (F["ub"], F["zb"]))):
                dve.wait_ge(sem("ev_act"), (c * 8 + (FFN_EV[l] + 2 * p + b + 1)))
                dve.scalar_tensor_tensor(z[:, 0:NPR], u[:, 1:1 + NPR], ffn_vec(l, "w_ffn_conv", 1, f + b * FT),
                                         z[:, 0:NPR], ALU.mult, ALU.add)
                dve.scalar_tensor_tensor(z[:, NPR:TOK], u[:, 2 + NPR:2 + TOK], ffn_vec(l, "w_ffn_conv", 2, f + b * FT),
                                         kslice(F["fsc"], f + b * FT), ALU.mult, ALU.add)
                dve.tensor_copy(kslice(F["utail"], f + b * FT), u[:, NPR:TOK + 2]).then_inc(sem("tail_ready"), 1)
                dve.drain()
                dve.scalar_tensor_tensor(z[:, 0:NPR], u[:, 0:NPR], ffn_vec(l, "w_ffn_conv", 0, f + b * FT),
                                         z[:, 0:NPR], ALU.mult, ALU.add).then_inc(sem("conv_done"), 1)

        def gated(c, p, n):
            dve.drain()
            dve.wait_ge(sem("gelu_ready"), n + 1)
            dve.tensor_tensor(F["g32"], F["gel"], F["zb"], ALU.mult)
            dve.drain()
            dve.tensor_copy(G[0][:, p, :], F["g32"])
            dve.drain()
            dve.tensor_tensor(G[1][:, p, :], F["g32"], G[0][:, p, :].bitcast(F32), ALU.subtract).then_inc(sem("g_ready"), 1)

        def sums_out(c, first):
            for n in range(KT):
                dve.wait_ge(sem("tile_done"), c * 16 + (D0 + 10 + n + 1 if not (first == "last") else D0 + 8 + n + 1))
                ps = PS[(D0 + n) % 2][:, :, 0:CH]
                dst = c3(O0[:, n, :])
                if first is True:
                    dve.tensor_copy(dst, ps).then_inc(sem("ev_dve"), 1)
                else:
                    dve.tensor_tensor(dst, dst, ps, ALU.add).then_inc(sem("ev_dve"), 1)

        def chunk(c):
            for p in range(PAIRS):
                n = c * PAIRS + (p + FT * l)
                f = c * PAIRS + p
                conv(c, p, n, f)
                if p == 0 and not (isinstance(c, int) and c == 0):
                    sums_out(c - 1, isinstance(c, int) and c == 1)
                gated(c, p, n)

        chunk(0)
        chunk(1)
        with dve.Fori(2, CHUNKS) as c:
            chunk(c)
        sums_out(CHUNKS - 1, "last")
        dve.drain()

    def ffn_pe(pe, tile, l):
        t0 = (T_FFN0, T_FFN1)[l]
        E0, V0, D0 = FFN_EV[l], 48 * l, FFN_DONE[l]

        def up(c, p, w):
            for b in range(2):
                pe.wait_ge(sem("w_split"), w + b + 1)
                if p == 1 and not (isinstance(c, int) and c == 0):
                    pe.wait_ge(sem("ev_dve"), c * 8 + (V0 + b - 1))
                else:
                    pe.wait_ge(sem("ev_act"), c * 8 + (E0 + 2 * p + b - 1))
                first = isinstance(c, int) and c == 0 and p == 0 and b == 0
                tile(None, (t0 + b) % 2, (D0 + b) % 2, HB, h0=(8, 32)[l] if first else None)

        def down(c, w, last_chunk=False):
            pe.wait_ge(sem("g_ready"), c * PAIRS + (PAIRS + FT * l))
            for d in range(4):
                pe.wait_ge(sem("w_split"), w + d + 1)
                for b in range(2):
                    if d == 0:
                        pe.wait_ge(sem("ev_act"), c * 8 + (E0 + b + (7 if last_chunk else 9)))
                    else:
                        pe.wait_ge(sem("ev_dve"), c * 8 + (V0 + 2 * d + b - 1))
                    tile(None, (t0 + d) % 2, (D0 + b) % 2, G, K=PAIRS, kw=256, off=b * P)

        for p in range(PAIRS):
            up(0, p, t0 + 2 * p)

        def chunk(c):
            w = (c - 1) * 12 + (t0 + 8)
            up(c, 0, w)
            down(c - 1, w + 2)
            for p in range(1, PAIRS):
                up(c, p, w + 4 + 2 * p)

        rolled(pe, 1, CHUNKS, chunk)
        down(CHUNKS - 1, t0 + 68, True)

    ROT = (4, 5, 8, 9)
    VAL = (6, 7, 10, 11)
    KV_EV, KV_DONE = 72, 120

    def aux_uses():
        use, at_use = {}, 0
        for n in range(12):
            use[n] = at_use
            if n in ROT + VAL:
                at_use += 3
        return use

    USE = aux_uses()
    PCD = [PC, PD]

    def kv_act(act):
        act.wait_ge(sem("x_spill"), 32)

        def out(n):
            if n in ROT:
                act.wait_ge(sem("kr_ready"), ROT.index(n) + 1)
                act.dma_start(o["kvT"][n], kr).then_inc(sem("kr_out"), 16)
            else:
                act.dma_start(o["kvT"][n], kb[n % 2]).then_inc(sem(f"kb_out{n % 2}"), 16)

        for n in range(12):
            act.wait_ge(sem("tile_done"), KV_DONE + n + 1)
            if n >= 2:
                act.wait_ge(sem("kb_used"), n - 1)
                outs = len([m for m in range(n % 2, n - 1, 2) if m not in ROT])
                act.wait_ge(sem(f"kb_out{n % 2}"), 16 * outs)
            act.activation(c3(kb[n % 2]), PS[n % 2][:, :, 0:CH], ACT.Copy).then_inc(sem("ev_act"), 1)
            if n in ROT:
                if n % 2:
                    out(n - 1)
                continue
            act.drain()
            if n - 1 in ROT:
                out(n - 1)
            out(n)

    def kv_pe(pe, tile):
        def aux(n):
            pe.wait_ge(sem("ev_act"), KV_EV + n + 1)
            for c in range(3):
                u = USE[n] + c
                if u >= 2:
                    pe.wait_ge(sem("aux_used"), u - 1)
                px = PCD[u % 2]
                if n in ROT:
                    mm = pe.matmul(px[:, 0:CH], perm, kb[n % 2][:, c * CH:(c + 1) * CH], start=True, stop=True)
                elif c < 2:
                    for i in range(4):
                        tok = (4 * c + i) * P
                        mm = pe.transpose(px[:, i * P:(i + 1) * P], kb[n % 2][:, tok:tok + P], ident)
                else:
                    mm = pe.transpose(px[0:NS, 0:P], kb[n % 2][:, NPR:TOK], ident)
                mm.then_inc(sem("aux_done"), 1)

        for n in range(12):
            pe.wait_ge(sem("w_split"), T_KV + n + 1)
            pe.wait_ge(sem("ev_act"), KV_EV + n - 1)
            tile(None, n % 2, n % 2, HB, h0=16 if n == 0 else None)
            if n >= 1 and n - 1 in ROT + VAL:
                aux(n - 1)
        aux(11)

    def kv_dve(dve):
        for b in range(2):
            dve.memset(KBD[b][0:64, :, 1, :], 0.0)
            dve.memset(KBD[b][64:128, :, 0, :], 0.0)
        for n in range(12):
            kind, t = n // 2, n % 2
            dve.wait_ge(sem("ev_act"), KV_EV + n + 1)
            if kind < 2:
                for half in range(2):
                    for par in range(2):
                        src = kb[n % 2][half * 64:half * 64 + 64, 0:NPR].rearrange("p (n m two) -> p m n two", m=8, two=2)
                        cp = dve.tensor_copy(K2[kind][par * 64:par * 64 + 64, :, 2 * t + half, :], src[:, :, :, par])
                cp.then_inc(sem("kb_used"), 1)
            elif n in ROT:
                b = kind // 4
                m = ROT.index(n)
                if m:
                    dve.wait_ge(sem("kr_out"), 16 * m)
                dve.drain()
                dve.tensor_tensor(kr, kb[n % 2], cosT, ALU.mult)
                for c in range(3):
                    u = USE[n] + c
                    dve.wait_ge(sem("aux_done"), u + 1)
                    cs = slice(c * CH, (c + 1) * CH)
                    dve.tensor_tensor(kx[:, cs], PCD[u % 2][:, 0:CH], sinT[:, cs], ALU.mult).then_inc(sem("aux_used"), 1)
                dve.drain()
                dve.tensor_tensor(kr, kr, kx, ALU.add).then_inc(sem("kr_ready"), 1)
                dve.drain()
                for half in range(2):
                    hs = slice(64 * half, 64 * half + 64)
                    dve.tensor_copy(KBD[b][hs, t, half, :], kr[hs, 0:NPR])
                dve.tensor_copy(k_new[:, b, t, :], kr[:, NPR:TOK]).then_inc(sem("kb_used"), 1)
            else:
                b = kind // 4
                for c in range(2):
                    u = USE[n] + c
                    dve.wait_ge(sem("aux_done"), u + 1)
                    dve.tensor_copy(VT[b][:, 4 * c:4 * c + 4, t * P:(t + 1) * P],
                                    PCD[u % 2].rearrange("p (i d) -> p i d", d=P)).then_inc(sem("aux_used"), 1)
                u = USE[n] + 2
                dve.wait_ge(sem("aux_done"), u + 1)
                dve.tensor_copy(v_new[0:NS, b, t * P:(t + 1) * P], PCD[u % 2][0:NS, 0:P]).then_inc(sem("aux_used"), 1)
                dve.drain()
                dve.tensor_copy(deps, deps).then_inc(sem("kb_used"), 1)

    def modulate_in_place(eng):
        if eng is nc.scalar:
            for k in range(KT):
                eng.wait_ge(sem("t_ready"), 24 + k + 1)
                eng.activation(HB[0][:, k, 0:NPR], X[:, k, 0:NPR], ACT.Identity, bias=mcol(6, k), scale=mcol(7, k))
                eng.drain()
                eng.activation(X[:, k, 0:NPR], X[:, k, 0:NPR], ACT.Identity, bias=mcol(6, k),
                               scale=mcol(7, k)).then_inc(sem("hi_done"), 1)
            return
        eng.wait_ge(sem("x_back"), 48)
        eng.wait_ge(sem("tile_done"), 132)
        sam = X[:, :, NPR:TOK]
        eng.tensor_tensor(ts, sam, rms[:, NPR:TOK].unsqueeze(1).broadcast_to([P, KT, NS]), ALU.mult)
        eng.drain()
        eng.tensor_tensor(ts, ts, msamp(7), ALU.mult)
        eng.drain()
        eng.tensor_tensor(ts, ts, msamp(6), ALU.add)
        eng.drain()
        eng.tensor_copy(HB[0][:, :, NPR:TOK], ts)
        eng.drain()
        eng.tensor_tensor(HB[1][:, :, NPR:TOK], ts, HB[0][:, :, NPR:TOK].bitcast(F32), ALU.subtract)
        for k in range(KT + 1):
            if k < KT:
                eng.tensor_tensor(X[:, k, 0:NPR], X[:, k, 0:NPR], rms[:, 0:NPR], ALU.mult).then_inc(sem("t_ready"), 1)
            if k >= 1:
                eng.wait_ge(sem("hi_done"), 24 + k)
                eng.tensor_tensor(HB[1][:, k - 1, 0:NPR], X[:, k - 1, 0:NPR], HB[0][:, k - 1, 0:NPR].bitcast(F32),
                                  ALU.subtract).then_inc(sem("h_ready"), 1)
        eng.drain()

    Q_EV, Q_DONE = 84, 132

    def q_pe(pe, tile):
        for n in range(9):
            pe.wait_ge(sem("w_split"), T_Q + n + 1)
            pe.wait_ge(sem("ev_act"), Q_EV + n - 1)
            if n == 0:
                pe.wait_ge(sem("aux_used"), 24)
            tile(None, n % 2, n % 2, HB, h0=24 if n == 0 else None)
        pe.wait_ge(sem("ev_act"), Q_EV + 9)
        for i in range(QT):
            mm = pe.transpose(PC[:, i * 48:(i + 1) * 48], rms[0:48, i * P:(i + 1) * P], ident[0:48, 0:48])
        pe.transpose(PD[0:NS, 0:48], rms[0:48, NPR:TOK], ident[0:48, 0:48]).then_inc(sem("gt_done"), 1)

    def q_act(act):
        for n in range(9):
            act.wait_ge(sem("tile_done"), Q_DONE + n + 1)
            if n < 8:
                act.activation(c3(X[:, n, :]), PS[n % 2][:, :, 0:CH], ACT.Copy).then_inc(sem("ev_act"), 1)
            else:
                act.activation(c3(rms), PS[n % 2][:, :, 0:CH], ACT.Tanh, scale=0.5).then_inc(sem("ev_act"), 1)

    def q_dve(dve):
        dve.wait_ge(sem("gt_done"), 1)
        dve.tensor_scalar(flat(gtok), PC[:, 0:QT * 48], 0.5, 0.5, ALU.mult, ALU.add)
        dve.tensor_scalar(gsmp, PD[0:NS, 0:48], 0.5, 0.5, ALU.mult, ALU.add).then_inc(sem("gates_ready"), 1)
        dve.drain()

    def compress_pe(pe, k2, ps):
        for kv in range(2):
            out = ps[kv][:, 0:260].rearrange("p (g c) -> p g c", c=65)
            for m in range(16):
                mm = pe.matmul(out[:, :, 1:65] if m < 8 else out[:, :, 0:64], C["w1k" if kv == 0 else "w1v"][:, m, :],
                               k2(kv, m % 8), start=(m == 0), stop=(m == 15), skip_group_check=True)
        return mm

    def hidden(ps):
        return ps[:, 0:260].rearrange("p (g c) -> p g c", c=65)[:, :, 1:64]

    def stage_c_pe(pe):
        pe.wait_ge(sem("cmp_in"), 16 * 4)
        pe.wait_ge(sem("gates_ready"), 1)
        for kv in range(2):
            for m in range(16):
                mm = pe.matmul(PD[:, kv:kv + 1], C["w1k" if kv == 0 else "w1v"][:, m, :], C["pe"][:, kv, m:m + 1],
                               start=(m == 0 and kv == 0), stop=(m == 15), skip_group_check=True)
        mm.then_inc(sem("pe_done"), 1)
        compress_pe(pe, lambda kv, m: K2[kv][:, m, :, :], [PA[:, 0, :], PA[:, 1, :]]).then_inc(sem("hid_done"), 1)
        pe.wait_ge(sem("hid_ready"), 1)
        for half in range(2):
            pe.matmul(PB[64 * half:64 * half + 64, 0, 0:126], C["w2"][:, 0, :],
                      C["hid"][:, 0, half:4:2, 0:63], start=True, stop=True)
        for half in range(2):
            for t in range(2):
                mm = pe.matmul(PB[64 * half:64 * half + 63, 1, t * 64:(t + 1) * 64], C["hid"][:, 1, 2 * t + half, 0:63],
                               C["w2"][:, 1, :], start=True, stop=True, skip_group_check=True)
        mm.then_inc(sem("kc_done"), 1)
        pe.wait_ge(sem("kc_ready"), 1)

        def scores(u):
            t, i = u // QT, u % QT
            if u >= 2:
                pe.wait_ge(sem("sc_read"), u - 1)
            for r in range(4):
                mm = pe.matmul(PA[:, u % 2, r * P:(r + 1) * P], X[:, t * 4 + r, i * P:(i + 1) * P],
                               C["kc"][:, t, :, :], start=(r == 0), stop=True, skip_group_check=True)
            mm.then_inc(sem("sc_done"), 1)

        scores(0)
        scores(1)
        for u in range(16):
            t = u // QT
            pe.wait_ge(sem("pg_ready"), u + 1)
            if u >= 2:
                pe.wait_ge(sem("ct_ready"), u - 1)
            for r in range(4):
                mm = pe.transpose(PB[:, u % 2, r * P:(r + 1) * P], pbuf[u % 2][:, 512 + r * P:512 + (r + 1) * P], ident)
            mm.then_inc(sem("ctr_done"), 1)
            if u + 2 < 16:
                scores(u + 2)
            pe.wait_ge(sem("ct_ready"), u + 1)
            if u >= 2:
                pe.wait_ge(sem("oc_done"), u - 1)
            pe.matmul(PCD[u % 2], C["vc"][:, t, :], flat(C["ct"]), start=True, stop=True).then_inc(sem("oc_mm"), 1)

    def stage_c_act(act):
        act.wait_ge(sem("hid_done"), 1)
        act.wait_ge(sem("b1_ready"), 1)
        for kv in range(2):
            g = act.activation(C["hid"][:, kv, :, 0:63], hidden(PA[:, kv, :]), ACT.Gelu_apprx_tanh, bias=C["b1c"][:, kv:kv + 1])
        g.then_inc(sem("hid_ready"), 1)
        def exps(u):
            sc = pbuf[u % 2][:, 0:512]
            act.wait_ge(sem("cs_ready"), u + 1)
            act.activation(sc, sc, ACT.Exp, scale=SCALE).then_inc(sem("ce_ready"), 1)

        exps(0)
        for u in range(16):
            t, i = u // QT, u % QT
            if u + 1 < 16:
                exps(u + 1)
            act.wait_ge(sem("ctr_done"), u + 1)
            after(act, sem("oc_mm"), u)
            act.activation(flat(C["ct"]), PB[:, u % 2, :], ACT.Copy).then_inc(sem("ct_ready"), 1)
            act.wait_ge(sem("oc_mm"), u + 1)
            act.activation(OC[:, t * 4:t * 4 + 4, i * P:(i + 1) * P], PCD[u % 2].rearrange("p (r n) -> p r n", n=P),
                           ACT.Copy).then_inc(sem("oc_done"), 1)

    def select_blocks(dve, im, out, top, im2, n, rows=P):
        for h in range(n):
            dve.max(top[0:rows, h, :], im[0:rows, h, :])
        dve.drain()
        for h in range(n):
            dve.match_replace(im2[0:rows, h, :], top[0:rows, h, :], im[0:rows, h, :], TAKEN)
        dve.drain()
        return dve.tensor_scalar(out, im2[0:rows], TAKEN, NEG, ALU.not_equal, ALU.mult)

    def stage_c_dve(dve):
        dve.memset(flat(C["kc"]), 0.0)
        dve.memset(flat(C["vc"]), 0.0)
        dve.wait_ge(sem("pe_done"), 1)
        dve.tensor_tensor(C["b1c"], PD[:, 0:2], vec[:, VC["b_cmp1"]:VC["b_cmp1"] + 2], ALU.add).then_inc(sem("b1_ready"), 1)
        dve.drain()
        dve.wait_ge(sem("kc_done"), 1)
        for half in range(2):
            hs = slice(64 * half, 64 * half + 64)
            vs = slice(64 * half, 64 * half + 63)
            dve.tensor_copy(C["kc"][hs, :, half, 0:63], PB[hs, 0, 0:126].rearrange("p (t n) -> p t n", n=63))
            cp = dve.tensor_copy(C["vc"][vs, :, 64 * half:64 * half + 64], PB[vs, 1, 0:128].rearrange("p (t n) -> p t n", n=64))
        cp.then_inc(sem("kc_ready"), 1)
        dve.wait_ge(sem("att_in"), 16 * 5)
        bc = lambda ap: ap.unsqueeze(1).broadcast_to([P, 8, 64])
        bn = lambda ap: ap.unsqueeze(2).broadcast_to([P, 8, 64])

        def shifted(u):
            s3 = pbuf[u % 2][:, 0:512].rearrange("p (h n) -> p h n", n=64)
            dve.wait_ge(sem("sc_done"), u + 1)
            if u >= 2:
                dve.wait_ge(sem("pg_ready"), u - 1)
            dve.tensor_tensor(s3, PA[:, u % 2, :].rearrange("p (h n) -> p h n", n=64), bc(C["cadd"][:, u % QT, :]),
                              ALU.add).then_inc(sem("sc_read"), 1)
            dve.drain()
            dve.tensor_reduce(C["cm"], s3, AXX, ALU.max)
            dve.drain()
            dve.tensor_tensor(s3, s3, bn(C["cm"]), ALU.subtract).then_inc(sem("cs_ready"), 1)
            dve.drain()

        shifted(0)
        for u in range(16):
            t, i = u // QT, u % QT
            pb = pbuf[u % 2]
            s3 = pb[:, 0:512].rearrange("p (h n) -> p h n", n=64)
            if u + 1 < 16:
                shifted(u + 1)
            dve.wait_ge(sem("ce_ready"), u + 1)
            if i == 0:
                dve.tensor_tensor(s3, s3, bc(C["cmul"][:, i, :]), ALU.mult)
                dve.drain()
            dve.tensor_reduce(C["cs"], s3, AXX, ALU.add)
            dve.drain()
            dve.tensor_scalar(C["cs"], C["cs"], 1e-30, None, ALU.max)
            dve.drain()
            dve.reciprocal(C["cs"], C["cs"])
            dve.drain()
            dve.tensor_tensor(s3, s3, bn(C["cs"]), ALU.mult).then_inc(sem("pc_done"), 1)
            dve.drain()
            dve.tensor_reduce(C["im0"], pb[:, 0:512].rearrange("p (r h n) -> p h n r", r=4, h=2), AXX, ALU.add)
            dve.drain()
            q4 = C["im0"].rearrange("p h (j q) -> p h j q", q=4)
            dve.tensor_reduce(C["im"], q4, AXX, ALU.add)
            dve.drain()
            dve.tensor_tensor(C["im"][:, :, 1:16], C["im"][:, :, 1:16], q4[:, :, 0:15, 3], ALU.add)
            dve.drain()
            mb = lambda ap: ap.unsqueeze(1).broadcast_to([P, 2, 16])
            dve.tensor_tensor(C["im"], C["im"], mb(C["m1"][:, i, :]), ALU.mult)
            dve.drain()
            dve.tensor_tensor(C["im"], C["im"], mb(C["m2"][:, i, :]), ALU.add)
            dve.drain()
            select_blocks(dve, C["im"], selm[:, 2 * t:2 * t + 2, i, :], C["top"], C["im2"], 2).then_inc(sem("sel_ready"), 1)
        dve.drain()

    def rotate_pe(pe):
        pe.wait_ge(sem("sc_read"), 16)
        pe.wait_ge(sem("ct_ready"), 16)
        for n in range(KT):
            if n >= 2:
                pe.wait_ge(sem("rot_read"), n - 1)
            for c in range(NCH):
                mm = pe.matmul(PS[n % 2][:, c, 0:CH], perm, X[:, n, c * CH:(c + 1) * CH], start=True, stop=True)
            mm.then_inc(sem("rot_mm"), 1)

    def rotate_dve(dve):
        dve.tensor_copy(ts, X[:, :, NPR:TOK])
        dve.drain()
        for n in range(KT):
            dve.wait_ge(sem("rot_mm"), n + 1)
            dve.tensor_tensor(c3(rx), PS[n % 2][:, :, 0:CH], c3(sinT), ALU.mult).then_inc(sem("rot_read"), 1)
            dve.tensor_tensor(X[:, n, :], X[:, n, :], cosT, ALU.mult)
            dve.drain()
            dve.tensor_tensor(X[:, n, :], X[:, n, :], rx, ALU.add).then_inc(sem("q_rotated"), 1)
            dve.drain()

    UNITS = [(t, i, b, half) for t in range(2) for i in range(QT) for b in range(2) for half in range(2)]
    NU = len(UNITS)
    AHEAD = 4

    def key_tiles(u):
        t, i, b, half = UNITS[u]
        return list(range(0 if b == 0 else max(0, i - 4), i + 1))

    GROUPS, OF_UNIT = [], []
    for _u in range(NU):
        _kt = key_tiles(_u)
        OF_UNIT.append([])
        for _p in range(0, len(_kt), 4):
            OF_UNIT[-1].append(len(GROUPS))
            GROUPS.append((_u, _p, _kt[_p:_p + 4]))
    NG = len(GROUPS)
    assert NG % 6 == 0

    def att_pe(pe):
        def scores(r, u):
            t, i, b, half = UNITS[u]
            kt = key_tiles(u)
            if u % 32 == 0:
                pe.wait_ge(sem("qc_ready"), r * 2 + u // 32 + 1)
            if u >= 2:
                pe.wait_ge(sem("max_done"), r * NU + u - 1)
            ps = PS[u % 2].rearrange("p c n -> p (c n)")
            for at_ in range(0, len(kt) * P, 512):
                n = min(512, len(kt) * P - at_)
                k0 = kt[0] * P + at_
                mm = pe.matmul(ps[:, at_:at_ + n], qc[t][:, i * P:(i + 1) * P], KBD[b][:, t, half, k0:k0 + n],
                               start=True, stop=True)
            mm.then_inc(sem("s_done"), 1)

        def transposes(r, g):
            u, p0, kt = GROUPS[g]
            if p0 == 0:
                pe.wait_ge(sem("p_ready"), r * NU + u + 1)
            if g >= 2:
                pe.wait_ge(sem("pt_ready"), r * NG + g - 1)
                v_, vp = GROUPS[g - 2][0], GROUPS[g - 2][1]
                if v_ % 4 == 0 and vp == 0 and v_ >= 8:
                    pe.wait_ge(sem("oc_added"), r * 16 + v_ // 4 - 1)
            for n in range(len(kt)):
                mm = pe.transpose(PCD[g % 2][:, n * P:(n + 1) * P], pbuf[u % 5][:, (p0 + n) * P:(p0 + n + 1) * P], ident)
            mm.then_inc(sem("t_done"), 1)

        def values(r, g):
            u, p0, kt = GROUPS[g]
            t, i, b, half = UNITS[u]
            j = u // 4
            if g >= NG - 2:
                pe.wait_ge(sem("pt_ready"), r * NG + g + 1)
                pe.matmul(PCD[g % 2][0:1, 0:1], ident[:, 0:1], ident[:, 0:1], start=True, stop=True, skip_group_check=True)
            for n, k in enumerate(kt):
                mm = pe.matmul(PS[j % 2][64 * half:64 * half + 64, 2, 0:P], VT[b][:, k, t * P + 64 * half:t * P + 64 * half + 64],
                               pt[g % 3][:, n * P:(n + 1) * P], start=(b == 0 and k == 0), stop=(b == 1 and k == i),
                               skip_group_check=True)
            mm.then_inc(sem("pv_done"), 1)

        def row(r):
            for s in range(NU + AHEAD):
                if s < NU:
                    scores(r, s)
                if s >= AHEAD:
                    for g in OF_UNIT[s - AHEAD]:
                        transposes(r, g)
                        if g >= 2:
                            values(r, g - 2)
            values(r, NG - 2)
            values(r, NG - 1)

        rolled(pe, 0, 4, row)

    def copy_out(eng, r, g):
        n = len(GROUPS[g][2]) * P
        eng.wait_ge(sem("t_done"), r * NG + g + 1)
        if g >= 3:
            eng.wait_ge(sem("pv_done"), r * NG + g - 2)
        eng.activation(pt[g % 3][:, 0:n], PCD[g % 2][:, 0:n], ACT.Copy).then_inc(sem("pt_ready"), 1)

    def att_act(act):
        act.wait_ge(sem("q_rotated"), KT)

        def row(r):
            for t in range(2):
                act.activation(qc[t], kslice(X, r + 4 * t)[:, 0:NPR], ACT.Copy).then_inc(sem("qc_ready"), 1)
            for s in range(NU + AHEAD):
                if 1 <= s <= NU:
                    u = s - 1
                    n = len(key_tiles(u)) * P
                    act.wait_ge(sem("max_done"), r * NU + u + 1)
                    act.activation(pbuf[u % 5][:, 0:n], pbuf[u % 5][:, 0:n], ACT.Exp, bias=nmx[u % 5], scale=-1.0,
                                   accum_out=psm[u % 5]).then_inc(sem("exp_done"), 1)
                if s >= AHEAD:
                    for g in OF_UNIT[s - AHEAD]:
                        copy_out(act, r, g)
            act.drain()

        rolled(act, 0, 4, row)

    def att_dve(dve):
        def maxima(r, u):
            t, i, b, half = UNITS[u]
            n = len(key_tiles(u))
            ps, pb = PS[u % 2].rearrange("p c n -> p (c n)"), pbuf[u % 5]
            dve.wait_ge(sem("s_done"), r * NU + u + 1)
            if u >= 5:
                dve.wait_ge(sem("t_done"), r * NG + OF_UNIT[u - 5][-1] + 1)
            dve.memset(dmark, 0.0)
            if b == 0 and i > 0:
                m = selm[:, 2 * t + half, i, 0:2 * i].unsqueeze(2).broadcast_to([P, 2 * i, 64])
                v3 = lambda ap: ap[:, 0:i * P].rearrange("p (j k) -> p j k", k=64)
                dve.tensor_tensor_reduce(v3(pb), v3(ps), m, -SCALE, 3e38, ALU.add, ALU.min, nm0)
                dve.drain()
                dve.tensor_tensor_reduce(pb[:, i * P:(i + 1) * P], ps[:, i * P:(i + 1) * P], wmask[:, 512:640], -SCALE,
                                         nm0, ALU.add, ALU.min, nmx[u % 5]).then_inc(sem("max_done"), 1)
            else:
                dve.tensor_tensor_reduce(pb[:, 0:n * P], ps[:, 0:n * P], wmask[:, 640 - n * P:640], -SCALE, 3e38,
                                         ALU.add, ALU.min, nmx[u % 5]).then_inc(sem("max_done"), 1)
            dve.drain()

        def add(r, j):
            t, i = j // QT, j % QT
            last = OF_UNIT[4 * j + 3][-1]
            dve.wait_ge(sem("pv_done"), r * NG + last + 1)
            dst = kslice(OC, r + 4 * t)[:, i * P:(i + 1) * P]
            dve.tensor_tensor(dst, dst, PS[j % 2][:, 2, 0:P], ALU.add).then_inc(sem("oc_added"), 1)

        def row(r):
            dve.tensor_copy(gcur.rearrange("p i b t h -> p i (b t) h"),
                            gtok[:, :, 16:48].rearrange("p i (bt r2) -> p i bt r2", r2=8)[:, :, :, ds(r * 2, 2)]).then_inc(sem("gcur_ready"), 1)
            dve.drain()
            for s in range(NU + AHEAD):
                if 2 <= s <= NU + 1:
                    dve.wait_ge(sem("exp_done"), r * NU + s - 1)
                    dve.reciprocal(psm[(s - 2) % 5], psm[(s - 2) % 5]).then_inc(sem("sum_inverted"), 1)
                if s < NU:
                    maxima(r, s)
                if s >= AHEAD:
                    u = s - AHEAD
                    if u % 4 == 1 and u > 1:
                        add(r, u // 4 - 1)
            add(r, NU // 4 - 1)
            dve.drain()

        rolled(dve, 0, 4, row)

    def stage_c_pool(pool):
        for u in range(16):
            t, i = u // QT, u % QT
            pb = pbuf[u % 2]
            pool.wait_ge(sem("pc_done"), u + 1)
            if u >= 2:
                pool.wait_ge(sem("ctr_done"), u - 1)
            pool.tensor_tensor(pb[:, 512:1024].rearrange("p (h n) -> p h n", n=64), pb[:, 0:512].rearrange("p (h n) -> p h n", n=64),
                               gtok[:, i, t * 8:t * 8 + 8].unsqueeze(2).broadcast_to([P, 8, 64]), ALU.mult).then_inc(sem("pg_ready"), 1)

    def att_pool(pool):
        def row(r):
            pool.wait_ge(sem("gcur_ready"), r + 1)
            for u in range(NU):
                t, i, b, half = UNITS[u]
                n = len(key_tiles(u)) * P
                pool.wait_ge(sem("sum_inverted"), r * NU + u + 1)
                pool.tensor_tensor(pmark, zero[0:1], zero[0:1], ALU.add)
                pool.tensor_scalar(pbuf[u % 5][:, 0:n], pbuf[u % 5][:, 0:n], gcur[:, i, b, t, half:half + 1], psm[u % 5],
                                   ALU.mult, ALU.mult).then_inc(sem("p_ready"), 1)
                pool.drain()

        rolled(pool, 0, 4, row)

    SR = NS * 16
    PG = 768
    FILL = (PAGES + 1) * 16

    def new_rows(pe, s, b, out, rhs_of):
        q = s // 2
        for t in range(2):
            mm = pe.matmul(out, qpad[b][:, s, t, :], rhs_of(t), start=(s % 2 == 0 and t == 0), stop=(s % 2 == 1 and t == 1),
                           skip_group_check=True)
        return mm

    def smp_pe(pe):
        pe.wait_ge(sem("oc_added"), 64)
        pe.wait_ge(sem("qpad_ready"), 2)
        pe.wait_ge(sem("smp_in"), 16 * 7)

        def rows(bank, c0, n, s):
            q = 32 * (s // 2)
            return bank[q:q + 32, c0:c0 + n]

        for q in range(0, NS, 2):
            for b in range(2):
                for s in (q, q + 1):
                    new_rows(pe, s, 1, rows(PA[:, 2, :], b, 1, s), lambda t: k_new[:, b, t, s:s + 1])
        for s in range(NS + 1):
            if s < NS:
                big = sbuf_s[s % 2]
                pe.wait_ge(sem(f"page_in{s % 2}"), FILL * (s // 2 + 1))
                if s:
                    pe.wait_ge(sem("shid_ready"), s)
                out = [PB[:, 1 + kv, 0:260].rearrange("p (g c) -> p g c", c=65) for kv in range(2)]
                for kv in range(2):
                    for m in range(16):
                        rhs = big[:, :, kv * 256 + (m % 8) * 32:kv * 256 + (m % 8) * 32 + 32].rearrange("p j (g b) -> p j g b", b=8)
                        dst = out[kv][:, :, 1:65] if m < 8 else out[kv][:, :, 0:64]
                        mm = pe.matmul(dst.rearrange("p g (j b) -> p j g b", b=8), (sw1k if kv == 0 else sw1v)[:, m, :],
                                       rhs, start=(m == 0), stop=(m == 15), skip_group_check=True)
                mm.then_inc(sem("shid_done"), 1)
            if s >= 1:
                pe.wait_ge(sem("shid_ready"), s)
                if s >= 2:
                    pe.wait_ge(sem("skc_ready"), s - 1)
                for half in range(2):
                    pe.matmul(PC[64 * half:64 * half + 64, 0:126], sw2[:, 0, :], shid[:, 0, half:4:2, 0:63], start=True,
                              stop=True, skip_group_check=True)
                for g in range(4):
                    mm = pe.matmul(PD[0:63, g * 64:(g + 1) * 64], shid[:, 1, g, 0:63], sw2[:, 1, :], start=True, stop=True,
                                   skip_group_check=True)
                mm.then_inc(sem("skc_done"), 1)
            if s < NS:
                for c in range(2):
                    new_rows(pe, s, 1, rows(PA[:, c, :], 0, 512, s), lambda t: big[:, 4 * c:4 * c + 4, 512 + t * P:512 + (t + 1) * P])
                new_rows(pe, s, 1, rows(PB[:, 0, :], 0, 512, s), lambda t: skw[s % 2][:, t, :]).then_inc(sem("page_used"), 1)
            if s >= 1:
                pe.wait_ge(sem("skc_ready"), s)
                mm = new_rows(pe, s - 1, 0, rows(PA[:, 2, :], 64, 63, s - 1), lambda t: kcs[:, t, :])
        mm.then_inc(sem("ss_done"), 1)
        pe.matmul(PD[:, 256:304], sE, gsmp, start=True, stop=True, skip_group_check=True).then_inc(sem("sgate_mm"), 1)
        pe.wait_ge(sem("pc_ready"), 1)
        pe.matmul(PC[:, 0:64], perm, s_c, start=True, stop=True).then_inc(sem("simp_mm"), 1)
        pe.wait_ge(sem("sp_ready"), 1)
        pe.transpose(PD[0:64, 0:P], s_c, ident).then_inc(sem("sT_done"), 1)
        pe.wait_ge(sem("sp_ready"), 2)
        for k in range(4):
            mm = pe.transpose(PC[:, k * P:(k + 1) * P], s_w[:, k * P:(k + 1) * P], ident)
        mm.then_inc(sem("sT_done"), 1)
        pe.wait_ge(sem("sp_ready"), 3)
        for k in range(8):
            mm = pe.transpose(PA[:, k // 4, (k % 4) * P:(k % 4 + 1) * P], s_s[:, k * P:(k + 1) * P], ident)
        for b in range(2):
            mm = pe.transpose(PB[0:NS, 1, b * P:(b + 1) * P], pnew[:, b, :], ident)
        mm.then_inc(sem("sT_done"), 1)
        pe.wait_ge(sem("pT_ready"), 1)
        out = PB[:, 0, 0:64].rearrange("p (s k) -> p s k", k=8)
        pe.wait_ge(sem("vwin_in"), 16 * NS)
        pe.wait_ge(sem("vall_in"), 16 * NS * PAGES)
        for g in range(4):
            t, half = g // 2, g % 2
            hs = slice(64 * half, 64 * half + 64)
            vs = slice(t * P + 64 * half, t * P + 64 * half + 64)
            for b in range(2):
                pe.matmul(out[hs, :, 4 * t:4 * t + 4], v_new[0:NS, b, vs],
                          pnT[:, b, :].rearrange("p (s h) -> p s h", h=16)[:, :, 4 * g:4 * g + 4],
                          start=(b == 0), stop=False, skip_group_check=True)
            for s in range(NS):
                o_ = out[hs, s, 4 * t:4 * t + 4]
                cs = slice(16 * s + 4 * g, 16 * s + 4 * g + 4)
                pe.matmul(o_, vcs[0:63, s, vs], pT[0:63, 12, cs], start=False, stop=False, skip_group_check=True)
                for k in range(4):
                    pe.matmul(o_, vwin[:, s, k, vs], pT[:, 8 + k, cs], start=False, stop=False, skip_group_check=True)
                for k in range(PAGES):
                    mm = pe.matmul(o_, vall[:, s, k, vs], pT[:, k, cs], start=False, stop=(k == PAGES - 1), skip_group_check=True)
        mm.then_inc(sem("so_done"), 1)

    def smp_act(act):
        for s in range(NS):
            act.wait_ge(sem("shid_done"), s + 1)
            if s:
                act.wait_ge(sem("skc_done"), s)
            for kv in range(2):
                gl = act.activation(shid[:, kv, :, 0:63], hidden(PB[:, 1 + kv, :]), ACT.Gelu_apprx_tanh,
                                    bias=C["b1c"][:, kv:kv + 1])
            gl.then_inc(sem("shid_ready"), 1)
        for n, (buf, w) in enumerate(((s_c, 63), (s_w, 513), (s_s, 1025))):
            act.wait_ge(sem("sneg_ready"), n + 1)
            act.activation(buf[:, 0:w], buf[:, 0:w], ACT.Exp, bias=snm[:, n:n + 1], scale=SCALE,
                           accum_out=ssum[:, n:n + 1]).then_inc(sem("sexp_done"), 1)
        act.wait_ge(sem("sT_done"), 3)
        act.activation(pT[:, 0:4, :].rearrange("p k n -> p (k n)"), PA[:, 0, :], ACT.Copy)
        act.activation(pT[:, 4:8, :].rearrange("p k n -> p (k n)"), PA[:, 1, :], ACT.Copy).then_inc(sem("pT_half"), 1)
        for k in range(KT):
            if k == 0:
                act.wait_ge(sem("so_copied"), 1)
            act.activation(HB[1][:, k, :], OC[:, k, :], ACT.Copy).then_inc(sem("o_hi"), 1)

    def smp_dve(dve):
        for b in range(2):
            dve.memset(flat(qpad[b]), 0.0)
        dve.drain()
        for b, src in enumerate((ts, X[:, :, NPR:TOK])):
            for s in range(NS):
                for t in range(2):
                    for half in range(2):
                        hs = slice(64 * half, 64 * half + 64)
                        c0 = 16 * (s % 2) + 8 * t + 4 * half
                        cp = dve.tensor_copy(qpad[b][hs, s, t, c0:c0 + 4], src[hs, 4 * t:4 * t + 4, s])
            cp.then_inc(sem("qpad_ready"), 1)
        for s in range(NS):
            dve.wait_ge(sem("skc_done"), s + 1)
            dve.tensor_copy(kcs, PC[:, 0:126].rearrange("p (t n) -> p t n", n=63))
            dve.tensor_copy(vcs[0:63, s, :], PD[0:63, 0:256]).then_inc(sem("skc_ready"), 1)
        dve.drain()

        def shifted(n, buf, w):
            dve.drain()
            dve.tensor_reduce(snm[:, n:n + 1], buf[:, 0:w], AXX, ALU.max)
            dve.drain()
            dve.tensor_scalar(snm[:, n:n + 1], snm[:, n:n + 1], -SCALE, None, ALU.mult).then_inc(sem("sneg_ready"), 1)

        def normalised(n, buf, w, gate):
            dve.wait_ge(sem("sexp_done"), n + 1)
            dve.reciprocal(ssum[:, n:n + 1], ssum[:, n:n + 1])
            dve.drain()
            return dve.tensor_scalar(buf[:, 0:w], buf[:, 0:w], ssum[:, n:n + 1], gate, ALU.mult, ALU.mult)

        dve.wait_ge(sem("ss_done"), 1)
        dve.memset(s_c[:, 63:64], 0.0)
        dve.tensor_copy(s_c[:, 0:63], PA[:, 2, 64:127])
        shifted(0, s_c, 63)
        dve.tensor_copy(s_w[:, 1:512], PB[:, 0, 1:512])
        dve.memset(s_w[:, 0:1], NEG)
        dve.tensor_copy(s_w[:, 512:513], PA[:, 2, 1:2])
        shifted(1, s_w, 513)
        dve.wait_ge(sem("sgate_mm"), 1)
        for b in range(3):
            dve.tensor_tensor(sg48[:, b, :], PD[:, 256 + b * 16:272 + b * 16], s_hm, ALU.mult)
        dve.drain()
        dve.tensor_reduce(sgate, sg48, AXX, ALU.add)
        dve.drain()
        normalised(0, s_c, 63, 1.0).then_inc(sem("pc_ready"), 1)
        dve.wait_ge(sem("simp_mm"), 1)
        dve.tensor_scalar(s_c[:, 0:63], s_c[:, 0:63], sgate[:, 0:1], None, ALU.mult).then_inc(sem("sp_ready"), 1)
        q4 = PC[:, 0:64].rearrange("p (j q) -> p j q", q=4)
        dve.tensor_reduce(sim_[:, 0:16], q4, AXX, ALU.add)
        dve.drain()
        dve.tensor_tensor(sim_[:, 1:16], sim_[:, 1:16], q4[:, 0:15, 3], ALU.add)
        dve.drain()
        dve.memset(sim_[:, 0:1], FORCED)
        dve.memset(sim_[:, 15:17], FORCED)
        normalised(1, s_w, 513, sgate[:, 2:3])
        dve.drain()
        dve.tensor_scalar(pnew[:, 1, :], s_smp, s_w[:, 512:513], None, ALU.mult).then_inc(sem("sp_ready"), 1)
        select_blocks(dve, sim_.unsqueeze(1), ssel.unsqueeze(1), stop_.unsqueeze(1), sim2.unsqueeze(1), 1)
        dve.drain()
        dve.tensor_tensor(s_s[:, 0:1024].rearrange("p (j k) -> p j k", k=64), PA[:, 0:2, :].rearrange("p c (j k) -> p (c j) k", k=64),
                          ssel[:, 0:16].unsqueeze(2).broadcast_to([P, 16, 64]), ALU.add)
        dve.tensor_copy(s_s[:, 1024:1025], PA[:, 2, 0:1])
        shifted(2, s_s, 1025)
        normalised(2, s_s, 1025, sgate[:, 1:2])
        dve.drain()
        dve.tensor_scalar(pnew[:, 0, :], s_smp, s_s[:, 1024:1025], None, ALU.mult).then_inc(sem("sp_ready"), 1)
        dve.wait_ge(sem("sT_done"), 3)
        dve.tensor_copy(pT[0:64, 12, :], PD[0:64, 0:P])
        dve.tensor_copy(pT[:, 8:12, :].rearrange("p k n -> p (k n)"), PC)
        dve.tensor_copy(pnT, PB[0:NS, 1, 0:2 * P].rearrange("p (b n) -> p b n", n=P))
        dve.wait_ge(sem("pT_half"), 1)
        dve.drain()
        dve.memset(dmark, 0.0).then_inc(sem("pT_ready"), 1)
        dve.wait_ge(sem("so_done"), 1)
        dve.tensor_copy(OC[:, :, NPR:TOK], PB[:, 0, 0:64].rearrange("p (s k) -> p k s", k=8)).then_inc(sem("so_copied"), 1)
        dve.drain()
        for k in range(KT):
            dve.wait_ge(sem("o_hi"), k + 1)
            dve.tensor_tensor(HB[0][:, k, :], OC[:, k, :], HB[1][:, k, :].bitcast(F32), ALU.subtract).then_inc(sem("o_ready"), 1)
        dve.drain()

    def smp_sp(sp):
        sp.wait_ge(sem("q_rotated"), KT)
        sp.dma_start(ptab, a["page_table"]).then_inc(sem("ptab_in"), 16)
        for dst, n in ((sw1k, "w1k"), (sw2, "w2"), (perm, "rowsum"), (sE, "rows"), (s_hm, "head_of_row"), (s_smp, "sample_of_row")):
            sp.dma_start(flat(dst), a[n]).then_inc(sem("smp_in"), 16)
        sp.wait_ge(sem("ptab_in"), 16)

        def pages(s, src, dst, name):
            for j in range(PAGES):
                page = sp.value_load(ptab[0:1, s * PAGES + j:s * PAGES + j + 1], min_val=0, max_val=NPHYS - 1)
                sp.dma_start(dst(j), a[src][ds(page, 1)].rearrange("o p n -> (o p) n")).then_inc(sem(name), 16)

        for s in range(NS):
            if s == 1:
                sp.wait_ge(sem("oc_added"), 64)
                sp.wait_ge(sem("qpad_ready"), 2)
                sp.dma_start(flat(sw1v), a["w1v"]).then_inc(sem("smp_in"), 16)
            if s >= 2:
                sp.wait_ge(sem("page_used"), s - 1)
            pages(s, "pages", lambda j: sbuf_s[s % 2][:, j, :], f"page_in{s % 2}")
            sp.dma_start(flat(skw[s % 2]), a["kwin"][s]).then_inc(sem(f"page_in{s % 2}"), 16)
            if s >= 1:
                pages(s - 1, "pages_v", lambda j: vall[:, s - 1, j, :], "vall_in")
        pages(NS - 1, "pages_v", lambda j: vall[:, NS - 1, j, :], "vall_in")
        sp.wait_ge(sem("page_used"), NS - 1)
        for s in range(NS):
            sp.dma_start(vwin[:, s, :, :].rearrange("p k n -> p (k n)"), a["vwin"][s]).then_inc(sem("vwin_in"), 16)

    @block.sync
    def _(sp):
        for dst, src in ((vec, a["vec"]), (ident, a["ident"]), (ones, a["ones"]), (perm, a["perm"]),
                         (cosT, a["cos"]), (sinT, a["sin"]), (cT, a["cT"]), (fold, a["fold"])):
            sp.dma_start(dst, src).then_inc(sem("const_in"), 16)

        def mod_weights(i):
            for b in range(4):
                after(sp, sem("mw_split"), i * 4 + b - 3)
                src = a["mw"][i * 4 + b] if isinstance(i, int) else a["mw"][ds(i * 4 + b, 1)].rearrange("o p n -> (o p) n")
                sp.dma_start(mw[b], src).then_inc(sem(f"mw_in{b}"), 16)

        rolled(sp, 0, 7, mod_weights)
        sp.dma_start(X[:, 0:4, :].rearrange("p k t -> p (k t)"), a["xT"][:, 0:4 * TOK]).then_inc(sem("x_in"), 16)
        sp.wait_ge(sem("mw_split"), 28)
        sp.dma_start(X[:, 4:8, :].rearrange("p k t -> p (k t)"), a["xT"][:, 4 * TOK:8 * TOK]).then_inc(sem("x_in"), 16)

        def tile_load(t, b):
            after(sp, sem("w_split"), t - 1)
            src = a["w"][t] if isinstance(t, int) else a["w"][ds(t, 1)].rearrange("o p n -> (o p) n")
            sp.dma_start(w_raw[b], src).then_inc(sem(f"w_in{b}"), 16)

        def stream(t0, t1):
            n = (t1 - t0) // 2
            if n:
                rolled(sp, 0, n, lambda i: [tile_load(i * 2 + t0 + c, (t0 + c) % 2) for c in range(2)])
            if (t1 - t0) % 2:
                tile_load(t1 - 1, (t1 - 1) % 2)

        sp.wait_ge(sem("t_ready"), 8)
        sp.wait_ge(sem("h_ready"), 8)
        sp.dma_start(L["lst"].rearrange("p a b c -> p (a b c)"), a["lst"]).then_inc(sem("st_in"), 16)
        sp.dma_start(L["lh0"].rearrange("p a b -> p (a b)"), a["lh0"]).then_inc(sem("st_in"), 16)

        def lru_weights(j):
            tile_load(j * 2, 0)
            tile_load(j * 2 + 1, 1)
            after(sp, sem("gate_mm"), j * 3)
            src = a["gw"][j] if isinstance(j, int) else a["gw"][ds(j, 1)].rearrange("o p n -> (o p) n")
            sp.dma_start(L["gw"], src).then_inc(sem("gw_in"), 16)

        rolled(sp, 0, KT, lru_weights)
        stream(T_LRUO, T_FFN0)
        sp.wait_ge(sem("s_ready"), KT)
        sp.dma_start(o["lru_tail"], L["ltail"].rearrange("p a b -> p (a b)")).then_inc(sem("out_lru"), 16)
        sp.dma_start(o["lru_h"], L["hlast"].rearrange("p a b -> p (a b)")).then_inc(sem("out_lru"), 16)
        sp.wait_ge(sem("out_lru"), 32)
        sp.dma_start(X.rearrange("p k t -> p (k t)"), a["xT"]).then_inc(sem("x_back"), 16)

        def ffn_loads(l, t0, x_done, h_done):
            stream(t0, t0 + 2)
            sp.wait_ge(sem("x_ready"), x_done)
            sp.dma_start(x_dram, X.rearrange("p k t -> p (k t)")).then_inc(sem("x_spill"), 16)
            sp.wait_ge(sem("h_ready"), h_done)
            sp.wait_ge(sem("x_spill"), (16, 48)[l])
            sp.dma_start(F["fst"].rearrange("p a b c -> p (a b c)"), a[f"fst{l}"]).then_inc(sem("st_in"), 16)
            stream(t0 + 2, t0 + 72)
            sp.wait_ge(sem("g_ready"), FT * (l + 1))
            sp.wait_ge(sem("tail_ready"), 2 * FT * (l + 1))
            sp.dma_start(o[f"ffn_tail{l}"], F["utail"].rearrange("p a b -> p (a b)")).then_inc(sem("out_ffn"), 16)
            sp.wait_ge(sem("out_ffn"), 16 * (l + 1))
            sp.dma_start(X.rearrange("p k t -> p (k t)"), x_dram).then_inc(sem("x_back"), 16)

        for n in ("kwin", "vwin", "lst", "fst0", "fst1"):
            sp.dma_start(o[n], a[n]).then_inc(sem("out_copy"), 16)
        ffn_loads(0, T_FFN0, 8, 16)
        stream(T_KV, T_KV + 2)
        sp.wait_ge(sem("x_ready"), 16)
        sp.dma_start(x_dram, X.rearrange("p k t -> p (k t)")).then_inc(sem("x_spill"), 16)
        stream(T_KV + 2, T_Q)
        sp.wait_ge(sem("kb_used"), 12)
        sp.wait_ge(sem("kr_out"), 16 * 4)
        sp.wait_ge(sem("kb_out0"), 16 * 4)
        sp.wait_ge(sem("kb_out1"), 16 * 4)
        sp.dma_start(X[:, 0:4, :].rearrange("p k t -> p (k t)"), x_dram[:, 0:4 * TOK]).then_inc(sem("x_back"), 16)
        stream(T_Q, T_O)
        sp.wait_ge(sem("tile_done"), 141)
        for dst, n in ((C["w1k"], "w1k"), (C["w1v"], "w1v"), (C["w2"], "w2"), (C["pe"], "pe"), (C["cadd"], "cadd"),
                       (C["cmul"], "cmul"), (C["m1"], "m1"), (C["m2"], "m2"), (wmask, "wmask")):
            sp.dma_start(flat(dst), a[n]).then_inc(sem("cmp_in" if n in ("w1k", "w1v", "w2", "pe") else "att_in"), 16)
        smp_sp(sp)
        sp.wait_ge(sem("so_done"), 1)
        sp.dma_start(X.rearrange("p k t -> p (k t)"), x_dram).then_inc(sem("x_back"), 16)
        stream(T_O, T_FFN1)
        ffn_loads(1, T_FFN1, 24, 40)
        for k in range(KT):
            sp.wait_ge(sem("x_ready"), 24 + k + 1)
            sp.dma_start(o["y"][:, k * TOK:(k + 1) * TOK], X[:, k, :]).then_inc(sem("out_y"), 16)
        sp.wait_ge(sem("out_y"), 16 * KT)
        sp.wait_ge(sem("out_copy"), 16 * 5)
        sp.wait_ge(sem("kr_out"), 16 * 4)
        sp.wait_ge(sem("kb_out0"), 16 * 4)
        sp.wait_ge(sem("kb_out1"), 16 * 4)
        sp.wait_ge(sem("out_lru"), 32)
        sp.wait_ge(sem("out_ffn"), 32)
    @block.gpsimd
    def _(pool):
        def split(t, b, landed, done):
            pool.wait_ge(sem(f"w_in{b}"), landed)
            after(pool, sem("tile_done"), done)
            pool.tensor_tensor(w_hi[b], w_raw[b], zero.broadcast_to([P, 1024]), ALU.add)
            pool.drain()
            pool.tensor_tensor(w_lo[b], w_raw[b], w_hi[b].bitcast(F32), ALU.subtract).then_inc(sem("w_split"), 1)

        def splits(t0, n, d0):
            rolled(pool, 0, n // 2, lambda i: [split(None, (t0 + c) % 2, i * 16 + 16 * ((t0 + c) // 2 + 1),
                                                     i * 2 + (d0 + c - 1)) for c in range(2)])
            if n % 2:
                split(None, (t0 + n - 1) % 2, 16 * ((t0 + n - 1) // 2 + 1), d0 + n - 2)

        def ffn_splits(t0, d0):
            splits(t0, 8, d0)
            done = [-1, 0, 1, 2, 4, 6, 8, 10, 11, 12, 13, 14]
            rolled(pool, 1, CHUNKS, lambda c: [split(None, (t0 + i) % 2, c * 96 + 16 * ((t0 + 8 - 12 + i) // 2 + 1),
                                                     c * 16 + (d0 - 8 + done[i])) for i in range(12)])
            for i, d in enumerate((-1, 0, 2, 4)):
                split(None, (t0 + i) % 2, 16 * ((t0 + 68 + i) // 2 + 1), d0 + 88 + d)

        pool.memset(zero, 0.0)
        pool.drain()
        splits(T_LRU, 24, 0)
        ffn_splits(T_FFN0, 24)
        splits(T_KV, 12, 120)
        splits(T_Q, 9, 132)
        stage_c_pool(pool)
        att_pool(pool)
        splits(T_O, 8, 141)
        ffn_splits(T_FFN1, 149)

    @block.scalar
    def _(act):
        act.wait_ge(sem("const_in"), 16 * 8)
        act.activation(csil.rearrange("p k c -> p (k c)"), cT, ACT.Silu).then_inc(sem("csil_ready"), 1)

        def mod_hi(i, b):
            act.wait_ge(sem(f"mw_in{b}"), (i + 1) * 16)
            after(act, sem("mod_mm"), i * 4 + b - 1)
            act.activation(mw_hi[:, b % 2, :], mw[b], ACT.Copy).then_inc(sem("mw_hi"), 1)

        def mod_rows(i):
            for b in range(4):
                act.wait_ge(sem("mod_mm"), i * 4 + b + 1)
                after(act, sem("mod_tr"), i * 4 + b - 1)
                act.activation(mrow[:, b % 2, :], PA[0:2 * NC, b % 2, :], ACT.Copy).then_inc(sem("mod_row"), 1)
                if b < 2:
                    mod_hi(i, b + 2)
                elif not (isinstance(i, int) and i == 6):
                    mod_hi(i + 1, b - 2)

        mod_hi(0, 0)
        mod_hi(0, 1)
        rolled(act, 0, 6, mod_rows)
        mod_rows(6)
        act.wait_ge(sem("lru_prep"), 1)
        act.activation(sp2, ts[:, :, 0], ACT.Exp).then_inc(sem("exp_lam"), 1)

        def squares(n, src, ready, per_k):
            b = NB[NREG[n]]
            for k in range(KT):
                if per_k or k == 0:
                    act.wait_ge(ready[0], ready[1] + (k + 1 if per_k else 0))
                if k >= 2 :
                    act.wait_ge(sem("sq_used"), 8 * n + k - 1)
                act.activation(b[f"sq{k % 2}_{NREG[n]}"], src[:, k, :], ACT.Square).then_inc(sem("sq_ready"), 1)
            root(n)

        def root(n):
            act.wait_ge(sem("sq_used"), 8 * n + 8)
            act.activation(c3(rms), PA[:, :, 0:CH], ACT.Sqrt, bias=deps).then_inc(sem("sqrt_done"), 1)

        def modulate(hn, n, dst, scale, shift):
            b = NB[NREG[n]]
            for k in range(KT):
                act.wait_ge(sem("t_ready"), 8 * hn + k + 1)
                t, h = b[f"t{k % 2}_{NREG[n]}"], b[f"h{k % 2}_{NREG[n]}"]
                act.activation(dst[0][:, k, 0:NPR], t[:, 0:NPR], ACT.Identity, bias=mcol(shift, k), scale=mcol(scale, k))
                if k >= 2:
                    act.wait_ge(sem("h_ready"), 8 * hn + k - 1)
                act.activation(h[:, 0:NPR], t[:, 0:NPR], ACT.Identity, bias=mcol(shift, k),
                               scale=mcol(scale, k)).then_inc(sem("hi_done"), 1)

        squares(0, X, (sem("x_in"), 32), False)
        act.wait_ge(sem("prep_done"), 1)
        modulate(0, 0, HA, 1, 0)

        def lru_gates(j):
            for c in range(NCH):
                act.wait_ge(sem("gate_mm"), j * 3 + c + 1)
                act.activation(mark, deps[0:1, :], ACT.Copy)
                if c == 0:
                    after(act, sem("ti_used"), j)
                cs = slice(c * CH, (c + 1) * CH)
                act.activation(L["tr"][:, cs], PC[:, 0:CH], ACT.Tanh, bias=v("b_lru_gate", j), scale=0.5)
                act.activation(L["ti"][:, cs], PD[:, 0:CH], ACT.Tanh, bias=v("b_lru_gate", j + 8),
                               scale=0.5).then_inc(sem("gate_ev"), 1)
            act.drain()
            sc = sp2[:, j:j + 1] if isinstance(j, int) else sp2[:, ds(j, 1)]
            act.activation(L["tr"], L["tr"], ACT.Tanh, bias=sc, scale=sc).then_inc(sem("t3_ready"), 1)

        def lru_root(j):
            act.wait_ge(sem("a2_ready"), j + 1)
            act.activation(L["lq"], L["tr"], ACT.Sqrt, scale=-1.0).then_inc(sem("root_ready"), 1)

        def lru_y(j):
            act.drain()
            act.wait_ge(sem("tile_done"), j * 2 + 1)
            act.activation(mark, deps[0:1, :], ACT.Copy)
            act.activation(c3(kslice(Y, j)), PA[:, :, 0:CH], ACT.Gelu_apprx_tanh, bias=v("b_lru_in", j)).then_inc(sem("ev_act"), 1)

        def lru_u(j):
            act.drain()
            after(act, sem("u_used"), j)
            act.wait_ge(sem("tile_done"), j * 2 + 2)
            act.activation(mark, deps[0:1, :], ACT.Copy)
            act.activation(c3(L["lu"][:, 3:3 + TOK]), PB[:, :, 0:CH], ACT.Identity,
                           bias=v("b_lru_in", j + 8)).then_inc(sem("ev_act"), 1)
            act.drain()
            act.activation(L["uc"], L["lu"][:, 3:3 + TOK], ACT.Identity, bias=v("b_lru_conv", j),
                           scale=v("w_lru_conv", j + 24)).then_inc(sem("z_ready"), 1)

        act.wait_ge(sem("lru_prep"), 2)
        lru_y(0)
        lru_u(0)
        with act.Fori(1, KT) as j:
            lru_gates(j - 1)
            lru_y(j)
            lru_root(j - 1)
            lru_u(j)
        lru_gates(KT - 1)
        lru_root(KT - 1)

        def evacuate(dst, psum0, ev0, n):
            def pair(i):
                for b in range(2):
                    act.wait_ge(sem("tile_done"), i * 2 + psum0 + b + 1)
                    act.activation(c3(kslice(dst, i * 2 + b)), PS[(psum0 + b) % 2][:, :, 0:CH],
                                   ACT.Copy).then_inc(sem("ev_act"), 1)
            rolled(act, 0, n // 2, pair)

        evacuate(O1, 16, 16, KT)
        squares(1, O1, (sem("ev_act"), 16), True)
        squares(2, X, (sem("x_ready"), 0), True)
        modulate(1, 2, HB, 4, 3)
        ffn_act(act, 0)
        squares(3, O0, (sem("ev_dve"), CHUNKS * 8 - 8), True)
        squares(4, X, (sem("x_ready"), 8), True)
        modulate(2, 4, HB, 13, 12)
        kv_act(act)
        modulate_in_place(act)
        q_act(act)
        stage_c_act(act)
        att_act(act)
        smp_act(act)
        evacuate(O1, 141, 93, KT)
        squares(5, O1, (sem("ev_act"), 93), True)
        squares(6, X, (sem("x_ready"), 16), True)
        modulate(4, 6, HB, 10, 9)
        ffn_act(act, 1)
        squares(7, O0, (sem("ev_dve"), 48 + CHUNKS * 8 - 8), True)

    @block.tensor
    def _(pe):
        pe.wait_ge(sem("csplit_ready"), 1)

        def mod_chunks(i, half):
            for b in (2 * half, 2 * half + 1):
                pe.wait_ge(sem("mw_split"), i * 4 + b + 1)
                after(pe, sem("mod_row"), i * 4 + b - 1)
                for k in range(KT):
                    pe.matmul(PA[0:2 * NC, b % 2, :], csplit[:, k, :], mw_hi[:, b % 2, k * 512:(k + 1) * 512],
                              start=(k == 0), stop=(k == KT - 1), skip_group_check=True)
                for k in range(KT):
                    mm = pe.matmul(PA[0:NC, b % 2, :], csplit[:, k, 0:NC], mw_lo[:, b % 2, k * 512:(k + 1) * 512],
                                   start=False, stop=(k == KT - 1), skip_group_check=True)
                mm.then_inc(sem("mod_mm"), 1)
            for b in (2 * half, 2 * half + 1):
                pe.wait_ge(sem("mod_row"), i * 4 + b + 1)
                after(pe, sem("mod_done"), i * 4 + b - 1)
                for q in range(4):
                    mm = pe.matmul(PB[:, b % 2, q * NC:(q + 1) * NC], mrow[:, b % 2, q * P:(q + 1) * P], fold,
                                   start=True, stop=True, skip_group_check=True)
                mm.then_inc(sem("mod_tr"), 1)

        rolled(pe, 0, 7, lambda i: [mod_chunks(i, half) for half in range(2)])

        def sums(n, free=None):
            if free:
                pe.wait_ge(*free)
            for k in range(KT):
                pe.wait_ge(sem("sq_ready"), 8 * n + k + 1)
                b = NB[NREG[n]][f"sq{k % 2}_{NREG[n]}"]
                for c in range(NCH):
                    mm = pe.matmul(PA[:, c, 0:CH], ones, b[:, c * CH:(c + 1) * CH], start=(k == 0), stop=(k == KT - 1))
                mm.then_inc(sem("sq_used"), 1)

        def tile(t, ws, ps, acts, K=KT, kw=P, off=0, h0=None, between=None, hs="h_ready"):
            whi, wlo = w_hi[ws], w_lo[ws]
            for k in range(K):
                if h0 is not None:
                    pe.wait_ge(sem(hs), h0 + k + 1)
                w0 = k * kw + off
                for n, (w, x) in enumerate(((whi, acts[0]), (whi, acts[1]), (wlo, acts[0]))):
                    for c in range(NCH):
                        mm = pe.matmul(PS[ps][:, c, 0:CH], w[:, w0:w0 + P], x[:, k, c * CH:(c + 1) * CH],
                                       start=(k == 0 and n == 0), stop=(k == K - 1 and n == 2))
                if between and k >= KT - NCH:
                    between(k - (KT - NCH))
            mm.then_inc(sem("tile_done"), 1)

        sums(0)

        def gate_chunk(j, c):
            pe.wait_ge(sem("uc_ready"), j + 1)
            pe.wait_ge(sem("gw_in"), (j + 1) * 16)
            after(pe, sem("gate_ev"), j * 3 + c)
            x = L["uc"][:, c * CH:(c + 1) * CH]
            pe.matmul(PC[:, 0:CH], L["gw"][:, 0:P], x, start=True, stop=True)
            pe.matmul(PD[:, 0:CH], L["gw"][:, P:2 * P], x, start=True, stop=True).then_inc(sem("gate_mm"), 1)

        def lru_pair(j):
            for b in range(2):
                pe.wait_ge(sem("w_split"), j * 2 + b + 1)
                after(pe, sem("ev_act"), j * 2 + b - 1)
                first = isinstance(j, int)
                tile(None, b, b, HA, h0=0 if first and b == 0 else None,
                     between=None if first or b else lambda c: gate_chunk(j - 1, c))

        rolled(pe, 0, KT, lru_pair)
        for c in range(NCH):
            gate_chunk(KT - 1, c)

        def project(t0, p0, ev0, acts, n, ready):
            def pair(i):
                for b in range(2):
                    pe.wait_ge(sem("w_split"), i * 2 + t0 + b + 1)
                    after(pe, sem("ev_act"), i * 2 + ev0 + b - 1)
                    first = isinstance(i, int) and b == 0
                    tile(None, (t0 + b) % 2, (p0 + b) % 2, acts, h0=0 if first else None, hs=ready)
            rolled(pe, 0, n // 2, pair)

        project(T_LRUO, 16, 16, SS, KT, "s_ready")
        sums(1, (sem("ev_act"), 23))
        sums(2)
        ffn_pe(pe, tile, 0)
        sums(3, (sem("ev_dve"), CHUNKS * 8 - 1))
        sums(4)
        kv_pe(pe, tile)
        q_pe(pe, tile)
        stage_c_pe(pe)
        rotate_pe(pe)
        att_pe(pe)
        smp_pe(pe)
        project(T_O, 141, 93, [HB[1], HB[0]], KT, "o_ready")
        sums(5, (sem("ev_act"), 101))
        sums(6)
        ffn_pe(pe, tile, 1)
        sums(7, (sem("ev_dve"), 48 + CHUNKS * 8))

    @block.vector
    def _(dve):
        dve.memset(deps, D * EPS)
        dve.wait_ge(sem("const_in"), 16 * 8)
        dve.tensor_scalar(vec[:, VC["g_norm"]:VC["g_norm"] + 72], vec[:, VC["g_norm"]:VC["g_norm"] + 72],
                          32.0, None, ALU.mult)
        dve.tensor_scalar(vec[:, VC["b_lru_gate"]:VC["b_lru_gate"] + 16], vec[:, VC["b_lru_gate"]:VC["b_lru_gate"] + 16],
                          0.5, None, ALU.mult)
        lam = vec[:, VC["lam"]:VC["lam"] + 8]
        dve.tensor_scalar(ts[:, :, 1], lam, -1.0, 0.0, ALU.mult, ALU.max)
        dve.scalar_tensor_tensor(ts[:, :, 0], lam, -1.0, lam, ALU.mult, ALU.min).then_inc(sem("lru_prep"), 1)

        def mod_lo(i, b):
            dve.wait_ge(sem("mw_hi"), i * 4 + b + 1)
            dve.tensor_tensor(mw_lo[:, b % 2, :], mw[b], mw_hi[:, b % 2, :].bitcast(F32), ALU.subtract).then_inc(sem("mw_split"), 1)

        dve.wait_ge(sem("csil_ready"), 1)
        dve.tensor_copy(csplit[:, :, 0:NC], csil)
        dve.drain()
        dve.tensor_tensor(csplit[:, :, NC:2 * NC], csil, csplit[:, :, 0:NC].bitcast(F32), ALU.subtract).then_inc(sem("csplit_ready"), 1)

        def mod_tiles(i):
            for b in range(4):
                if b < 2:
                    mod_lo(i, b + 2)
                elif not (isinstance(i, int) and i == 6):
                    mod_lo(i + 1, b - 2)
                dve.wait_ge(sem("mod_tr"), i * 4 + b + 1)
                t = i * 16 + b * 4
                dst = modT[:, t:t + 4, :] if isinstance(i, int) else modT[:, ds(t, 4), :]
                bias = vec[:, t:t + 4] if isinstance(i, int) else vec[:, ds(t, 4)]
                dve.tensor_tensor(dst, PB[:, b % 2, 0:4 * NC].rearrange("p (q c) -> p q c", c=NC),
                                  bias.unsqueeze(2).broadcast_to([P, 4, NC]), ALU.add).then_inc(sem("mod_done"), 1)

        mod_lo(0, 0)
        mod_lo(0, 1)
        rolled(dve, 0, 6, mod_tiles)
        mod_tiles(6)
        dve.drain()
        for l in range(2):
            for which, g in ((1, 0), (2, 1), (4, 2), (5, 3)):
                m = modT[:, (6 * l + which) * KT:(6 * l + which + 1) * KT, :]
                gb = vb("g_norm", (4 * l + g) * KT, KT, NC)
                dve.scalar_tensor_tensor(m, m, 1.0 if which in (1, 4) else 0.0, gb, ALU.add, ALU.mult)
        m = modT[:, 13 * KT:14 * KT, :]
        dve.scalar_tensor_tensor(m, m, 1.0, vb("g_norm", 64, KT, NC), ALU.add, ALU.mult).then_inc(sem("prep_done"), 1)
        dve.wait_ge(sem("exp_lam"), 1)
        y, y2, acc = ts[:, :, 2], ts[:, :, 3], ts[:, :, 4]
        dve.tensor_scalar(y, sp2, 2.0, None, ALU.add)
        dve.drain()
        dve.reciprocal(y2, y)
        dve.drain()
        dve.tensor_tensor(y, sp2, y2, ALU.mult)
        dve.drain()
        dve.tensor_tensor(y2, y, y, ALU.mult)
        dve.drain()
        dve.tensor_scalar(acc, y2, 4.0 / 17, 4.0 / 15, ALU.mult, ALU.add)
        for n in (13, 11, 9, 7, 5, 3, 1):
            dve.drain()
            dve.tensor_tensor(acc, acc, y2, ALU.mult)
            dve.drain()
            dve.tensor_scalar(acc, acc, 4.0 / n, None, ALU.add)
        dve.drain()
        dve.tensor_tensor(acc, acc, y, ALU.mult)
        dve.drain()
        dve.scalar_tensor_tensor(sp2, ts[:, :, 1], 2.0, acc, ALU.mult, ALU.add)
        dve.drain()

        def rms_of(n):
            dve.wait_ge(sem("sqrt_done"), n + 1)
            dve.reciprocal(rms, rms)
            dve.drain()

        def normed_samples(src):
            dve.tensor_tensor(ts, src[:, :, NPR:TOK], rms[:, NPR:TOK].unsqueeze(1).broadcast_to([P, KT, NS]), ALU.mult)
            dve.drain()

        def modulate(hn, n, src, dst, scale, shift):
            b = NB[NREG[n]]
            rms_of(n)
            normed_samples(src)
            dve.tensor_tensor(ts, ts, msamp(scale), ALU.mult)
            dve.drain()
            dve.tensor_tensor(ts, ts, msamp(shift), ALU.add)
            dve.drain()
            dve.tensor_copy(dst[0][:, :, NPR:TOK], ts)
            dve.drain()
            dve.tensor_tensor(dst[1][:, :, NPR:TOK], ts, dst[0][:, :, NPR:TOK].bitcast(F32), ALU.subtract)
            for k in range(KT + 1):
                if k < KT:
                    if k >= 2:
                        dve.wait_ge(sem("hi_done"), 8 * hn + k - 1)
                    dve.tensor_tensor(b[f"t{k % 2}_{NREG[n]}"][:, 0:NPR], src[:, k, 0:NPR], rms[:, 0:NPR],
                                      ALU.mult).then_inc(sem("t_ready"), 1)
                if k >= 1:
                    dve.wait_ge(sem("hi_done"), 8 * hn + k)
                    dve.tensor_tensor(dst[1][:, k - 1, 0:NPR], b[f"h{(k - 1) % 2}_{NREG[n]}"][:, 0:NPR],
                                      dst[0][:, k - 1, 0:NPR].bitcast(F32), ALU.subtract).then_inc(sem("h_ready"), 1)
            dve.drain()

        def residual(r, n, src, gate):
            b = NB[NREG[n]]
            rms_of(n)
            dve.wait_ge(sem("x_back"), (16, 32, 64, 80)[r])
            normed_samples(src)
            dve.tensor_tensor(ts, ts, msamp(gate), ALU.mult)
            dve.drain()
            dve.tensor_tensor(X[:, :, NPR:TOK], X[:, :, NPR:TOK], ts, ALU.add)
            for k in range(KT + 1):
                if k < KT:
                    dve.tensor_tensor(b[f"t{k % 2}_{NREG[n]}"][:, 0:NPR], src[:, k, 0:NPR], rms[:, 0:NPR], ALU.mult)
                if k >= 1:
                    dve.scalar_tensor_tensor(X[:, k - 1, 0:NPR], b[f"t{(k - 1) % 2}_{NREG[n]}"][:, 0:NPR], mcol(gate, k - 1),
                                             X[:, k - 1, 0:NPR], ALU.mult, ALU.add).then_inc(sem("x_ready"), 1)
                dve.drain()

        modulate(0, 0, X, HA, 1, 0)

        dve.memset(L["lu"][:, 0:3], 0.0)
        dve.wait_ge(sem("st_in"), 32)
        tmp = L["lsc"]
        dve.tensor_tensor(tmp, L["lst"][:, :, 0, :], vb("w_lru_conv", 0, KT, NS), ALU.mult)
        for k in (1, 2):
            dve.tensor_tensor(ts, L["lst"][:, :, k, :], vb("w_lru_conv", 8 * k, KT, NS), ALU.mult)
            dve.drain()
            dve.tensor_tensor(tmp, tmp, ts, ALU.add)
            dve.drain()
        dve.tensor_tensor(tmp, tmp, vb("b_lru_conv", 0, KT, NS), ALU.add).then_inc(sem("lru_prep"), 1)
        dve.drain()

        def lru_conv(j):
            lu, uc = L["lu"], L["uc"]
            dve.wait_ge(sem("z_ready"), j + 1)
            dve.scalar_tensor_tensor(uc[:, 0:NPR], lu[:, 2:2 + NPR], v("w_lru_conv", j + 16), uc[:, 0:NPR], ALU.mult, ALU.add)
            dve.scalar_tensor_tensor(uc[:, NPR:TOK], lu[:, 3 + NPR:3 + TOK], v("w_lru_conv", j + 24),
                                     kslice(L["lsc"], j), ALU.mult, ALU.add)
            dve.tensor_copy(kslice(L["ltail"], j), lu[:, NPR:TOK + 3])
            dve.drain()
            dve.scalar_tensor_tensor(uc[:, 0:NPR], lu[:, 1:1 + NPR], v("w_lru_conv", j + 8), uc[:, 0:NPR], ALU.mult, ALU.add)
            dve.drain()
            dve.scalar_tensor_tensor(uc[:, 0:NPR], lu[:, 0:NPR], v("w_lru_conv", j), uc[:, 0:NPR], ALU.mult,
                                     ALU.add).then_inc(sem("uc_ready"), 1)

        def lru_decay(j):
            tr, ti, q, am, uc = (L[n] for n in ("tr", "ti", "lq", "am", "uc"))
            dve.wait_ge(sem("t3_ready"), j + 1)
            dve.tensor_scalar(q, tr, 1.0, None, ALU.add)
            dve.scalar_tensor_tensor(ti, ti, 1.0, uc, ALU.add, ALU.mult).then_inc(sem("u_used"), 1)
            dve.drain()
            dve.reciprocal(am, q)
            dve.drain()
            dve.scalar_tensor_tensor(am, tr, -2.0, am, ALU.mult, ALU.mult)
            dve.drain()
            dve.scalar_tensor_tensor(tr, am, 2.0, am, ALU.add, ALU.mult).then_inc(sem("a2_ready"), 1)
            dve.drain()
            dve.tensor_scalar(am, am, 1.0, None, ALU.add)
            dve.drain()

        def lru_state(j):
            ti, q, am, hs = L["ti"], L["lq"], L["am"], L["hs"]
            dve.wait_ge(sem("root_ready"), j + 1)
            dve.scalar_tensor_tensor(q, ti, 0.5, q, ALU.mult, ALU.mult).then_inc(sem("ti_used"), 1)
            dve.tensor_tensor(ts[:, 0, :], am[:, NPR:TOK], kslice(L["lh0"], j), ALU.mult)
            dve.drain()
            dve.tensor_tensor_scan(hs[:, 0:NPR], am[:, 0:NPR], q[:, 0:NPR], 0.0, ALU.mult, ALU.add)
            dve.tensor_tensor(hs[:, NPR:TOK], q[:, NPR:TOK], ts[:, 0, :], ALU.add)
            dve.drain()
            dve.tensor_copy(kslice(L["hlast"], j), hs[:, NPR - 1:TOK])
            dve.tensor_tensor(q, hs, kslice(Y, j), ALU.mult)
            dve.drain()
            dve.tensor_copy(kslice(SS[0], j), q)
            dve.drain()
            dve.tensor_tensor(kslice(SS[1], j), q, kslice(SS[0], j).bitcast(F32), ALU.subtract).then_inc(sem("s_ready"), 1)
            dve.drain()

        lru_conv(0)
        with dve.Fori(1, KT) as j:
            lru_decay(j - 1)
            lru_conv(j)
            lru_state(j - 1)
        lru_decay(KT - 1)
        lru_state(KT - 1)
        residual(0, 1, O1, 2)
        modulate(1, 2, X, HB, 4, 3)
        ffn_dve(dve, 0)
        residual(1, 3, O0, 5)
        modulate(2, 4, X, HB, 13, 12)
        kv_dve(dve)
        modulate_in_place(dve)
        q_dve(dve)
        stage_c_dve(dve)
        rotate_dve(dve)
        att_dve(dve)
        smp_dve(dve)
        residual(2, 5, O1, 8)
        modulate(4, 6, X, HB, 10, 9)
        ffn_dve(dve, 1)
        residual(3, 7, O0, 11)

    block.__exit__(None, None, None)


def _rows(v):
    return v.reshape(-1, P).T


def _tile(w):
    return w.reshape(KT, P, -1).transpose(1, 0, 2).reshape(P, -1)


def _ffn_tiles(w_in, w_out):
    def up(f):
        return [_tile(w_in[:, f * P:(f + 1) * P]), _tile(w_in[:, DFF + f * P:DFF + (f + 1) * P])]

    def down(c):
        return [w_out[c * 512:(c + 1) * 512, d * 256:(d + 1) * 256].reshape(PAIRS, P, 256).transpose(1, 0, 2).reshape(P, -1)
                for d in range(4)]

    tiles = []
    for c in range(CHUNKS):
        tiles += up(PAIRS * c)
        if c:
            tiles += down(c - 1)
        for p in range(1, PAIRS):
            tiles += up(PAIRS * c + p)
    return tiles + down(CHUNKS - 1)


def _constants():
    a = {"ident": np.eye(P, dtype=np.float32), "ones": np.ones((P, P), np.float32)}
    perm = np.zeros((P, P), np.float32)
    pos = np.concatenate([np.arange(NPR), np.full(NS, PAST)]).astype(np.float32)
    inv = np.power(np.float32(500000.0), -np.arange(8, dtype=np.float32) * np.float32(2.0 / 16)).astype(np.float32)
    ang = pos[None, :] * inv[:, None]
    cos, sin = np.ones((P, TOK), np.float32), np.zeros((P, TOK), np.float32)
    for h in (0, 64):
        for d in range(8):
            perm[h + 8 + d, h + d] = perm[h + d, h + 8 + d] = 1
            cos[h + d] = cos[h + 8 + d] = np.cos(ang[d])
            sin[h + d], sin[h + 8 + d] = -np.sin(ang[d]), np.sin(ang[d])
        for d in range(16, 64):
            perm[h + d, h + d] = 1
    a["fold"] = np.concatenate([np.eye(NC, dtype=np.float32)] * 2)
    a["perm"], a["cos"], a["sin"] = perm, cos, sin
    q = np.arange(P)[:, None, None] + P * np.arange(QT)[None, :, None]
    n = np.arange(64)[None, None, :]
    seen = (16 * n + 31 <= q) & (n < NCMP)
    a["cadd"] = np.where(seen, 0, NEG).astype(np.float32).reshape(P, -1)
    a["cmul"] = seen.astype(np.float32).reshape(P, -1)
    j, cur = np.arange(16)[None, None, :], q // 64
    forced, valid = (j == 0) | (j == cur) | (j == cur - 1), j <= cur
    a["m1"] = (valid & ~forced).astype(np.float32).reshape(P, -1)
    a["m2"] = np.where(valid, np.where(forced, FORCED, 0), NEG).astype(np.float32).reshape(P, -1)
    dq, dk = np.arange(P)[:, None], np.arange(P)[None, :]
    wm = np.zeros((P, 640), np.float32)
    wm[:, :P] = np.where(dk > dq, 0, NEG)
    wm[:, 512:] = np.where(dk <= dq, 0, NEG)
    a["wmask"] = wm
    row = np.arange(P)
    s, t, half, r = row // 16, row % 16 // 8, row % 8 // 4, row % 4
    a["sample_of_row"] = (s[:, None] == np.arange(NS)).astype(np.float32)
    a["rows"] = a["sample_of_row"].T
    a["head_of_row"] = ((t * 8 + r * 2 + half)[:, None] == np.arange(16)).astype(np.float32)
    a["rowsum"] = ((row // 4)[:, None] == (row // 4)).astype(np.float32)
    return a


def _layout(I):
    A = lambda n: np.asarray(I[n])
    a = _constants()
    a["vec"] = np.concatenate([_rows(A(n)) for n in (
        "b_mod", "b_mod_kv", "g_norm", "g_kv", "b_lru_in", "w_lru_conv", "b_lru_conv", "b_lru_gate", "lru_lambda",
        "w_ffn_conv", "b_ffn_conv", "b_cmp1")], axis=1)
    c = np.concatenate([A("c_prompt"), A("c_sample")], 0)
    a["cT"] = c.T.reshape(KT, P, NC).transpose(1, 0, 2).reshape(P, KT * NC)
    wm = np.concatenate([A("w_mod")[0], A("w_mod")[1], A("w_mod_kv")], 1)
    a["mw"] = wm.reshape(KT, P, 28, 512).transpose(2, 1, 0, 3).reshape(28, P, 4096)
    x = np.concatenate([A("x_prompt")[0], A("x_sample")[:, 0]], 0)
    a["xT"] = x.T.reshape(KT, P, TOK).transpose(1, 0, 2).reshape(P, -1)
    a["lst"] = A("state_lru_conv")[0].reshape(NS, 3, KT, P).transpose(3, 2, 1, 0).reshape(P, -1)
    a["lh0"] = A("state_lru_h")[0].reshape(NS, KT, P).transpose(2, 1, 0).reshape(P, -1)
    a["gw"] = A("w_lru_gate")[0].transpose(1, 2, 0, 3).reshape(8, P, 256)
    for l in range(2):
        a[f"fst{l}"] = A("state_ffn_conv")[l].reshape(NS, 2, 48, P).transpose(3, 2, 1, 0).reshape(P, -1)
    w = A("w_lru_in")[0]
    tiles = []
    for j in range(KT):
        tiles += [_tile(w[:, j * P:(j + 1) * P]), _tile(w[:, D + j * P:D + (j + 1) * P])]
    tiles += [_tile(A("w_lru_out")[0][:, j * P:(j + 1) * P]) for j in range(KT)]
    tiles += _ffn_tiles(A("w_ffn_in")[0], A("w_ffn_out")[0])
    tiles += [_tile(A("w_kv")[:, n * P:(n + 1) * P]) for n in range(12)]
    w = A("w_nsa_qg")[0]
    heads = [np.r_[(8 * t + r) * 64:(8 * t + r) * 64 + 64, (8 * t + 4 + r) * 64:(8 * t + 4 + r) * 64 + 64]
             for t in range(2) for r in range(4)]
    tiles += [_tile(w[:, q]) for q in heads]
    gates = [D + (8 * t + 4 * h + r) * 3 + b for b in range(3) for t in range(2) for r in range(4) for h in range(2)]
    tiles += [_tile(np.concatenate([w[:, gates], np.zeros((D, 80), np.float32)], 1))]
    w = A("w_nsa_out")[0][np.concatenate(heads)]
    tiles += [_tile(w[:, j * P:(j + 1) * P]) for j in range(KT)]
    tiles += _ffn_tiles(A("w_ffn_in")[1], A("w_ffn_out")[1])
    a["w"] = np.stack(tiles)
    w = A("w_cmp1")
    for kv, n in ((0, "w1k"), (1, "w1v")):
        a[n] = w[kv].reshape(16, P, P).transpose(1, 0, 2).reshape(P, -1)
    a["w2"] = A("w_cmp2").transpose(1, 0, 2).reshape(P, -1)
    a["pe"] = A("pe_cmp").reshape(2, 16, P).transpose(2, 0, 1).reshape(P, -1)
    c = A("cache_nsa_kv")
    by_block = [c[:, :, kv].reshape(NPHYS, 8, 8, 2, 4, 64).transpose(0, 3, 5, 2, 4, 1).reshape(NPHYS, P, 256) for kv in range(2)]
    a["pages"] = np.concatenate(by_block + [c[:, :, 2].reshape(NPHYS, P, 2, 2, 64).transpose(0, 3, 4, 2, 1).reshape(NPHYS, P, 256)], 2)
    a["pages_v"] = c[:, :, 3].reshape(NPHYS, P, 256)
    w = A("state_nsa_win")
    a["kwin"] = w[:, :, 0].reshape(NS, 512, 2, 2, 64).transpose(0, 3, 4, 2, 1).reshape(NS, P, 1024)
    a["vwin"] = w[:, :, 1].reshape(NS, 4, P, 256).transpose(0, 2, 1, 3).reshape(NS, P, 1024)
    a["page_table"] = A("page_table").reshape(1, NS * PAGES)
    return {n: np.ascontiguousarray(v) for n, v in a.items()}


OUTS = {"y": (P, KT * TOK), "kvT": (12, P, TOK), "kwin": (NS, P, 1024), "vwin": (NS, P, 1024), "lru_h": (P, KT * NC),
        "lru_tail": (P, KT * 11), "lst": (P, KT * 3 * NS), "ffn_tail0": (P, 480), "ffn_tail1": (P, 480),
        "fst0": (P, 768), "fst1": (P, 768)}


def _arrange(g):
    y = g["y"].reshape(P, KT, TOK).transpose(2, 1, 0).reshape(TOK, D)
    kv = g["kvT"].reshape(6, 256, TOK).transpose(2, 0, 1).reshape(TOK, 6, 4, 64)
    k_old = g["kwin"].reshape(NS, 2, 64, 2, 512).transpose(0, 4, 3, 1, 2).reshape(NS, 512, 4, 64)
    v_old = g["vwin"].reshape(NS, P, 4, 256).transpose(0, 2, 1, 3).reshape(NS, 512, 4, 64)
    win_s = np.concatenate([np.stack([k_old, v_old], 2)[:, 1:], kv[NPR:, None, 4:]], 1)
    h = g["lru_h"].reshape(P, KT, NC).transpose(2, 1, 0).reshape(NC, D)
    tail = g["lru_tail"].reshape(P, KT, 11).transpose(2, 1, 0).reshape(11, D)
    old = g["lst"].reshape(P, KT, 3, NS).transpose(3, 2, 1, 0).reshape(NS, 3, D)
    conv_s = np.concatenate([old[:, 1:], tail[3:, None]], 1)
    fp, fs = [], []
    for l in range(2):
        t = g[f"ffn_tail{l}"].reshape(P, 48, 10).transpose(2, 1, 0).reshape(10, 2 * DFF)
        old = g[f"fst{l}"].reshape(P, 48, 2, NS).transpose(3, 2, 1, 0).reshape(NS, 2, 2 * DFF)
        fp.append(t[None, :2])
        fs.append(np.concatenate([old[:, 1:], t[2:, None]], 1))
    return (y[None, :NPR], y[NPR:, None], kv[None, :NPR, :4], kv[NPR:, None, :4], kv[None, NPR - 512:NPR, 4:], win_s,
            h[None, :1], h[None, 1:], tail[None, None, :3], conv_s[None], np.stack(fp), np.stack(fs))


def kernel(**inputs):
    import numpy as _np
    import concourse.bacc as _bacc
    from concourse import mybir as _mybir
    from concourse.bass_utils import run_bass_kernel_spmd as _run

    nc = _bacc.Bacc("TRN2", target_bir_lowering=False, num_devices=1)
    arrays, a, o = {}, {}, {}
    for name, v in _layout(inputs).items():
        arrays[f"in_{name}"] = v
        a[name] = nc.dram_tensor(f"in_{name}", v.shape, _mybir.dt.from_np(v.dtype), kind="ExternalInput").ap()
    for name, shape in OUTS.items():
        o[name] = nc.dram_tensor(f"out_{name}", shape, F32, kind="ExternalOutput").ap()
    build(nc, a, o)
    r = _run(nc, [arrays], core_ids=[0])
    return tuple(_np.ascontiguousarray(v) for v in _arrange({n: r.results[0][f"out_{n}"] for n in OUTS}))
```
